# Optimizing a Trainium2 kernel written in Bass

```python
import math
import jax, jax.numpy as jnp
from jax import lax
import numpy as np

D_MODEL = 2048
BATCH = 1
SEQ = 512
DEPTH = 2

D_MIX = D_MODEL
BR = D_MIX // 4
CONV_A_WIDTH = 3
ATT_HEADS = 8
ATT_HEAD_DIM = BR // ATT_HEADS
DILATIONS = ((128, 1), (512, 4), (2048, 16))
BLK = 128
REL_BUCKETS = 32
REL_MAX_DIST = 2048
LRU_HEADS = 8
LRU_HEAD_DIM = BR // LRU_HEADS
CONV_C_WIDTH = 4
LRU_C = 8.0
S5_CH = 16
S5_GROUPS = BR // S5_CH
S5_STATE = 64
N_IN = 4 * BR + 4 * BR + 2 * BR + 2 * BR
ALPHA = (2 * DEPTH) ** 0.25
BETA = (8 * DEPTH) ** -0.25
LN_EPS = 1e-5

kernel_name = "hybrid_parallel_conv_dilattn_rglru_s5"

def layer_norm(x, g, b):
    xf = x.astype(jnp.float32)
    mu = jnp.mean(xf, axis=-1, keepdims=True)
    var = jnp.mean(jnp.square(xf - mu), axis=-1, keepdims=True)
    return ((xf - mu) * lax.rsqrt(var + LN_EPS)).astype(x.dtype) * g + b

def causal_dwconv(x, w):
    K = w.shape[0]
    S = x.shape[1]
    xp = jnp.pad(x, ((0, 0), (K - 1, 0), (0, 0)))
    y = xp[:, :S] * w[0]
    for j in range(1, K):
        y = y + xp[:, j:j + S] * w[j]
    return y

def t5_bucket(dist):
    max_exact = REL_BUCKETS // 2
    nf = jnp.maximum(dist, 1).astype(jnp.float32)
    large = max_exact + (jnp.log(nf / max_exact) / math.log(REL_MAX_DIST / max_exact)
                         * (REL_BUCKETS - max_exact)).astype(jnp.int32)
    large = jnp.minimum(large, REL_BUCKETS - 1)
    return jnp.where(dist < max_exact, dist, large)

def dilated_group(q, k, v, rel_bias, window, dil):
    Bsz, S, H, hd = q.shape
    span = window // dil
    assert span <= BLK
    unit = dil * BLK
    S_pad = -(-S // unit) * unit
    nb = S_pad // unit
    pad = ((0, 0), (0, S_pad - S), (0, 0), (0, 0))

    def split(t):
        return jnp.pad(t, pad).reshape(Bsz, nb, BLK, dil, H, hd)

    def with_prev(t):
        prev = jnp.pad(t, ((0, 0), (1, 0), (0, 0), (0, 0), (0, 0), (0, 0)))[:, :-1]
        return jnp.concatenate([prev, t], axis=2)

    qb = split(q)
    kk = with_prev(split(k))
    vv = with_prev(split(v))
    s = jnp.einsum('bnirhd,bnjrhd->bnrhij', qb, kk).astype(jnp.float32)

    i = jnp.arange(BLK)[:, None]
    j = jnp.arange(2 * BLK)[None, :]
    delta = i + BLK - j
    bucket = t5_bucket(jnp.clip(delta, 0, span) * dil)
    bias = jnp.transpose(rel_bias[bucket], (2, 0, 1)).astype(jnp.float32)
    valid = (delta >= 0) & (delta <= span)
    has_prev = (jnp.arange(nb)[:, None, None] > 0) | (j >= BLK)[None]
    mask = valid[None] & has_prev

    s = jnp.where(mask[None, :, None, None], s + bias, -1e30)
    m = jnp.max(s, axis=-1, keepdims=True)
    p = jnp.exp(s - m)
    l = jnp.sum(p, axis=-1, keepdims=True)
    o = jnp.einsum('bnrhij,bnjrhd->bnirhd', (p / l).astype(v.dtype), vv)
    lse = (m + jnp.log(l))[..., 0]
    lse = jnp.transpose(lse, (0, 1, 4, 2, 3)).reshape(Bsz, S_pad, H)[:, :S]
    o = o.reshape(Bsz, S_pad, H, hd)[:, :S]
    return o, lse

def dilated_attention(q, k, v, rel_bias):
    outs, lses = [], []
    for window, dil in DILATIONS:
        o, lse = dilated_group(q, k, v, rel_bias, window, dil)
        outs.append(o)
        lses.append(lse)
    w = jax.nn.softmax(jnp.stack(lses, axis=0), axis=0)
    return jnp.einsum('gbsh,gbshd->bshd', w.astype(q.dtype), jnp.stack(outs, axis=0))

def linear_combine(e1, e2):
    a1, b1 = e1
    a2, b2 = e2
    return a1 * a2, a2 * b1 + b2

def complex_combine(e1, e2):
    ar1, ai1, br1, bi1 = e1
    ar2, ai2, br2, bi2 = e2
    return (ar2 * ar1 - ai2 * ai1,
            ar2 * ai1 + ai2 * ar1,
            ar2 * br1 - ai2 * bi1 + br2,
            ar2 * bi1 + ai2 * br1 + bi2)

def rglru_branch(xb, conv_w, conv_b, wa, ba, wx, bx, lam):
    Bsz, S, _ = xb.shape
    xc = causal_dwconv(xb, conv_w) + conv_b
    xh = xc.reshape(Bsz, S, LRU_HEADS, LRU_HEAD_DIM)
    r = jax.nn.sigmoid(jnp.einsum('bshi,hij->bshj', xh, wa).reshape(Bsz, S, BR) + ba)
    ig = jax.nn.sigmoid(jnp.einsum('bshi,hij->bshj', xh, wx).reshape(Bsz, S, BR) + bx)
    log_a = -LRU_C * r * jax.nn.softplus(-lam)
    a = jnp.exp(log_a)
    mult = jnp.sqrt(-jnp.expm1(2.0 * log_a))
    _, h = lax.associative_scan(linear_combine, (a, mult * ig * xc), axis=1)
    return h

def s5_branch(u, lam_re, lam_im, log_dt, b_re, b_im, c_re, c_im, d_skip, w_glu, b_glu):
    Bsz, S, _ = u.shape
    ug = u.reshape(Bsz, S, S5_GROUPS, S5_CH)
    dt = jnp.exp(log_dt)[:, None]
    mag = jnp.exp(lam_re * dt)
    ab_re = mag * jnp.cos(lam_im * dt)
    ab_im = mag * jnp.sin(lam_im * dt)
    den = lam_re * lam_re + lam_im * lam_im
    f_re = ((ab_re - 1.0) * lam_re + ab_im * lam_im) / den
    f_im = (ab_im * lam_re - (ab_re - 1.0) * lam_im) / den
    bb_re = f_re[..., None] * b_re - f_im[..., None] * b_im
    bb_im = f_re[..., None] * b_im + f_im[..., None] * b_re
    bu_re = jnp.einsum('bsgc,gpc->bsgp', ug, bb_re)
    bu_im = jnp.einsum('bsgc,gpc->bsgp', ug, bb_im)
    a_re = jnp.broadcast_to(ab_re, bu_re.shape)
    a_im = jnp.broadcast_to(ab_im, bu_im.shape)
    _, _, x_re, x_im = lax.associative_scan(complex_combine, (a_re, a_im, bu_re, bu_im), axis=1)
    y = jnp.einsum('gcp,bsgp->bsgc', c_re, x_re) - jnp.einsum('gcp,bsgp->bsgc', c_im, x_im)
    y = y.reshape(Bsz, S, BR) + d_skip * u
    y = jax.nn.gelu(y)
    return y * jax.nn.sigmoid(y @ w_glu + b_glu)

def setup_inputs(seed: int = 0) -> dict:
    key = jax.random.key(seed)
    ks = jax.random.split(key, 32)

    def nrm(k, shape, scale):
        return scale * jax.random.normal(k, shape, jnp.float32)

    HD = LRU_HEAD_DIM
    a_c = jax.random.uniform(ks[13], (DEPTH, BR), jnp.float32, minval=0.9, maxval=0.999)
    a0 = a_c ** (1.0 / LRU_C)
    lru_lambda = jnp.log(a0) - jnp.log1p(-a0)
    n_idx = jnp.arange(S5_STATE, dtype=jnp.float32)
    return {
        "x": nrm(ks[0], (BATCH, SEQ, D_MODEL), 1.0),
        "c": nrm(ks[1], (BATCH, D_MODEL), 1.0),
        "rel_bias": nrm(ks[2], (REL_BUCKETS, ATT_HEADS), 0.5),
        "w_ada": nrm(ks[3], (DEPTH, D_MODEL, 3 * D_MODEL), 0.1 * D_MODEL ** -0.5),
        "b_ada": nrm(ks[4], (DEPTH, 3 * D_MODEL), 0.01),
        "w_in": nrm(ks[5], (DEPTH, D_MODEL, N_IN), D_MODEL ** -0.5),
        "conv_a": nrm(ks[6], (DEPTH, CONV_A_WIDTH, BR), CONV_A_WIDTH ** -0.5),
        "conv_c": nrm(ks[7], (DEPTH, CONV_C_WIDTH, BR), CONV_C_WIDTH ** -0.5),
        "conv_c_b": nrm(ks[8], (DEPTH, BR), 0.01),
        "lru_wa": nrm(ks[9], (DEPTH, LRU_HEADS, HD, HD), HD ** -0.5),
        "lru_ba": nrm(ks[10], (DEPTH, BR), 0.01),
        "lru_wx": nrm(ks[11], (DEPTH, LRU_HEADS, HD, HD), HD ** -0.5),
        "lru_bx": nrm(ks[12], (DEPTH, BR), 0.01),
        "lru_lambda": lru_lambda,
        "s5_lam_re": -0.5 + nrm(ks[14], (DEPTH, S5_GROUPS, S5_STATE), 0.01),
        "s5_lam_im": jnp.pi * n_idx + nrm(ks[15], (DEPTH, S5_GROUPS, S5_STATE), 0.01),
        "s5_log_dt": jax.random.uniform(ks[16], (DEPTH, S5_GROUPS), jnp.float32,
                                        minval=math.log(1e-3), maxval=math.log(1e-1)),
        "s5_b_re": nrm(ks[17], (DEPTH, S5_GROUPS, S5_STATE, S5_CH), (2 * S5_CH) ** -0.5),
        "s5_b_im": nrm(ks[18], (DEPTH, S5_GROUPS, S5_STATE, S5_CH), (2 * S5_CH) ** -0.5),
        "s5_c_re": nrm(ks[19], (DEPTH, S5_GROUPS, S5_CH, S5_STATE), (2 * S5_STATE) ** -0.5),
        "s5_c_im": nrm(ks[20], (DEPTH, S5_GROUPS, S5_CH, S5_STATE), (2 * S5_STATE) ** -0.5),
        "s5_d": nrm(ks[21], (DEPTH, BR), 1.0),
        "s5_w_glu": nrm(ks[22], (DEPTH, BR, BR), BR ** -0.5),
        "s5_b_glu": nrm(ks[23], (DEPTH, BR), 0.01),
        "w_out": nrm(ks[24], (DEPTH, D_MIX, D_MODEL), BETA * D_MIX ** -0.5),
        "ln_g": 1.0 + nrm(ks[25], (DEPTH, D_MODEL), 0.01),
        "ln_b": nrm(ks[26], (DEPTH, D_MODEL), 0.01),
    }

def reference(x, c, rel_bias, w_ada, b_ada, w_in, conv_a, conv_c, conv_c_b, lru_wa, lru_ba,
              lru_wx, lru_bx, lru_lambda, s5_lam_re, s5_lam_im, s5_log_dt, s5_b_re, s5_b_im,
              s5_c_re, s5_c_im, s5_d, s5_w_glu, s5_b_glu, w_out, ln_g, ln_b):
    Bsz, S, _ = x.shape
    cond = jax.nn.silu(c)
    for l in range(DEPTH):
        ada = cond @ w_ada[l] + b_ada[l]
        shift, scale, gate = jnp.split(ada, 3, axis=-1)
        h = x * (1.0 + scale[:, None]) + shift[:, None]
        proj = h @ w_in[l]
        pa, pb, pc, pd = jnp.split(proj, [4 * BR, 8 * BR, 10 * BR], axis=-1)

        a_b, a_c, a_x, a_g = jnp.split(pa, 4, axis=-1)
        y_a = a_b * causal_dwconv(a_c * a_x, conv_a[l]) * jax.nn.silu(a_g)

        q, k, v, b_g = jnp.split(pb, 4, axis=-1)
        q = q.reshape(Bsz, S, ATT_HEADS, ATT_HEAD_DIM) * (ATT_HEAD_DIM ** -0.5)
        k = k.reshape(Bsz, S, ATT_HEADS, ATT_HEAD_DIM)
        v = v.reshape(Bsz, S, ATT_HEADS, ATT_HEAD_DIM)
        y_b = dilated_attention(q, k, v, rel_bias).reshape(Bsz, S, BR) * jax.nn.silu(b_g)

        c_x, c_g = jnp.split(pc, 2, axis=-1)
        y_c = rglru_branch(c_x, conv_c[l], conv_c_b[l], lru_wa[l], lru_ba[l], lru_wx[l],
                           lru_bx[l], lru_lambda[l]) * jax.nn.silu(c_g)

        d_u, d_g = jnp.split(pd, 2, axis=-1)
        y_d = s5_branch(d_u, s5_lam_re[l], s5_lam_im[l], s5_log_dt[l], s5_b_re[l], s5_b_im[l],
                        s5_c_re[l], s5_c_im[l], s5_d[l], s5_w_glu[l], s5_b_glu[l]) * jax.nn.silu(d_g)

        y = jnp.concatenate([y_a, y_b, y_c, y_d], axis=-1) @ w_out[l]
        x = layer_norm(ALPHA * x + (1.0 + gate[:, None]) * y, ln_g[l], ln_b[l])
    return x


_drawn_inputs = setup_inputs


def setup_inputs(seed=0):
    import zlib

    import numpy as np

    out = dict(_drawn_inputs(seed))
    spreads = {}
    factors = {'rel_bias': 4.56,
     'b_ada': 6.671,
     'conv_c_b': 8.0,
     'lru_ba': 64.0,
     'lru_bx': 64.0,
     's5_lam_re': 64.0,
     's5_lam_im': 64.0,
     's5_log_dt': 64.0,
     's5_b_re': 64.0,
     's5_b_im': 64.0,
     's5_c_re': 64.0,
     's5_c_im': 64.0,
     's5_w_glu': 3.497,
     's5_b_glu': 200.0,
     'ln_g': 3.83,
     'ln_b': 3.887}
    for name, (base, spread) in spreads.items():
        noise = np.random.default_rng([zlib.crc32(name.encode()), seed]).standard_normal(out[name].shape)
        drawn = base * np.exp(spread * noise) if base else spread * noise
        out[name] = __import__('jax').numpy.asarray(drawn.astype(out[name].dtype))
    for name, factor in factors.items():
        out[name] = (out[name] * factor).astype(out[name].dtype)
    return out
```

```python
import math
from contextlib import ExitStack

import numpy as np
import concourse.bass as bass
from concourse import mybir

F32 = mybir.dt.float32
F32R = mybir.dt.float32r
I32 = mybir.dt.int32
ALU = mybir.AluOpType
ACT = mybir.ActivationFunctionType
AX_X = mybir.AxisListType.X

P = 128
D = 2048
S = 512
DEPTH = 2
BR = D // 4
KT = D // P
CT = BR // P
ST = S // P
N_IN = 12 * BR
HEADS = 8
HD = BR // HEADS
CH = 16
GR = BR // CH
NS = 64
SQ = 4
TC = P
ALPHA = (2 * DEPTH) ** 0.25
EPS = 1e-5
NEG = -1e30
ROUND = 12582912.0
TWO_PI = 6.2831845
LRU_C = 8.0
GELU_C = math.sqrt(2 / math.pi)

UNITS = ("d_u", "c_x", "q", "k", "v", "c_g", "d_g", "a_c", "a_x", "b_g", "a_g", "a_b")
COLUMN = dict(a_b=0, a_c=1, a_x=2, a_g=3, q=4, k=5, v=6, b_g=7, c_x=8, c_g=9, d_u=10, d_g=11)
HALF = 2 * len(UNITS)
KH = KT // 2
NRAW, NHL = 3, 2
W_LOOP = CT * HALF
W_OUT = 32
ADA_RING = 4
ADA_CHUNKS = (((0, 32), (1, 0), (1, 16)), ((1, 32),))
OWN_STEPS = (168, 167)

ROWS = {}
_n = 0
for _name, _rows in (("conv_a", 12), ("conv_c", 16), ("conv_c_b", 4), ("lru_ba", 4), ("lru_bx", 4),
                     ("lru_lambda", 4), ("s5_d", 4), ("s5_b_glu", 4), ("ln_g", 16), ("ln_b", 16),
                     ("s5_lam_re", 16), ("s5_lam_im", 16)):
    ROWS[_name] = (_n, _rows)
    _n += _rows
N_ROWS = _n


def bucket_of(d):
    if d < 16:
        return d
    return min(31, 16 + int(np.float32(math.log(d / 16) / math.log(128)) * np.float32(16)))


def ada_group(layer, last):
    chunks = range(len(ADA_CHUNKS[layer]))
    return chunks if layer else chunks[1:] if last else chunks[:1]


class Signal:

    def __init__(self, sem, per=0, first=0):
        self.sem, self.per, self.first, self.local = sem, per, first, 0

    def at(self, n, step=0):
        return step * self.per + (self.first + n)


class Line:

    def __init__(self, eng):
        self.eng, self.step, self.last = eng, 0, None

    def __call__(self, ins, sig, n=1):
        ins.then_inc(sig.sem, n)
        sig.local += n
        self.last = sig
        return ins

    def settle(self):
        self.eng.wait_ge(self.last.sem, self.last.at(self.last.local, self.step))

    def enter(self, step, *sigs):
        self.step = step
        for s in sigs:
            s.local = 0


def trunk(nc, A, out):
    x_norm = nc.dram_tensor("x_norm_scratch", (S, D), F32, kind="Internal").ap()
    bias_row_d = nc.dram_tensor("bias_row_scratch", (HEADS, 640), F32, kind="Internal").ap()
    bias_d = nc.dram_tensor("bias_tile_scratch", (HEADS, P, S), F32, kind="Internal").ap()

    with ExitStack() as ctx:
        def sb(name, shape, dt=F32):
            return ctx.enter_context(nc.sbuf_tensor(name, shape, dt))

        def signal(name, per=0, first=0):
            return Signal(ctx.enter_context(nc.semaphore(name)), per, first)

        op_hi = sb("op_hi", [P, KT, S], F32R)
        op_lo = sb("op_lo", [P, KT, S], F32R)
        y_t = sb("y_t", [P, KT, S])
        z = y_t[:, :, :].rearrange("p (s n) t -> p s (n t)", s=ST)
        raw = sb("raw", [P, NRAW, KH * P])
        w_hi = sb("w_hi", [P, NHL, KH * P], F32R)
        w_lo = sb("w_lo", [P, NHL, KH * P], F32R)
        ada_in = sb("ada_in", [P, ADA_RING, S])
        ada_acc = sb("ada_acc", [P, 2, S])
        work = sb("work", [P, 24, S])
        bias_t = sb("bias_t", [P, 2, S])
        rot = sb("rot", [P, 2, SQ, TC])
        s5_w = sb("s5_w", [P, 4, P])
        s5_raw = sb("s5_raw", [P, 4, 64])
        s5_bb = sb("s5_bb", [P, 2, SQ, 2, CH])
        s5_cc = sb("s5_cc", [P, 2, 2, 64])
        s5_k = sb("s5_k", [P, 4, SQ])
        lru_w = sb("lru_w", [P, 2, P])
        xp = sb("xp", [P, 3 + S])
        va = sb("va", [P, 2 + S])
        ident = sb("ident", [P, P])
        ones = sb("ones", [P, P])
        j_row = sb("j_row", [P, TC])
        par = sb("par", [P, DEPTH, N_ROWS])
        ada_b = sb("ada_b", [P, DEPTH, 64])
        dt_in = sb("dt_in", [16, 2])
        dt_t = sb("dt_t", [P, DEPTH, 16])
        mask = sb("mask", [P, 4])
        ada_t = sb("ada_t", [P, DEPTH, 48])
        cond = sb("cond", [P, 16])
        s5c = sb("s5c", [P, DEPTH, 4, 16])
        lru_c = sb("lru_c", [P, DEPTH, 12])
        glu_hb = sb("glu_hb", [P, DEPTH, 4])
        hs = sb("hs", [P, 2, KT])
        gate1 = sb("gate1", [P, KT])
        tmp = sb("tmp", [P, 8, 16])
        rel = sb("rel", [HEADS, 32])
        soft = sb("soft", [P, 4, 4])
        carry = sb("carry", [P, 4])
        spare = sb("spare", [P, 1])
        stats = sb("stats", [P, ST, 4, 6])
        mv = sb("mv", [P, ST, 4])
        consts = sb("consts", [P, 2])

        u_d, xc, q_t, k_t, v_t = (work[:, i, :] for i in range(5))
        s5_s = [work[:, 5 + i, :] for i in range(5)]
        w_glu = work[:, 5:9, :]
        v_s = work[:, 10, :].rearrange("p (k d) -> p k d", k=ST)
        prob = work[:, 11:14, :].rearrange("p a b -> p (a b)")
        lru_s = [work[:, 11 + i, :] for i in range(3)]
        p_t = work[:, 14:16, :]
        gx = work[:, 16:18, :]
        gt = work[:, 18:20, :]
        silu_d = work[:, 20:24, :]
        ax = xp[:, 3:3 + S]
        gel = v_t
        gate_b = work[:, 0:4, :]
        glu_t = work[:, 14:18, :]
        ln_prev = work[:, 4:12, :].rearrange("p (i a) b -> p i (a b)", i=2)
        ln_last = work[:, 14:22, :].rearrange("p (i a) b -> p i (a b)", i=2)
        mix = work[:, 13, :]
        hf = work[:, 16:18, :]
        diag = work[:, 18:20, :]
        brow = work[0:HEADS, 16:19, :].rearrange("p a b -> p (a b)")[:, 0:1280].rearrange("p (a b) -> p a b", a=2)
        rows = work[:, 20, 0:2 * P].rearrange("p (a b) -> p a b", a=2)
        flip, mask_row, dt_row = work[:, 21, 0:P], work[0:32, 21, P:2 * P], work[0:16, 21, 2 * P:3 * P]
        j_int = work[:, 22, 0:TC].bitcast(I32)
        P_AT = [0, 128, 384, 768]
        bank = [ctx.enter_context(nc.psum_tensor(f"bank{i}", [P, S], F32)) for i in range(8)]

        const_done = signal("const_done")
        setup_dma = signal("setup_dma")
        row_dma = [signal(f"row_dma{l}") for l in range(DEPTH)]
        turned = signal("turned")
        setup_own = signal("setup_own")
        bias_own = signal("bias_own")
        setup_dve = signal("setup_dve")
        setup_act = signal("setup_act")
        bias_row = signal("bias_row")
        bias_io = signal("bias_io")
        bias_mm = signal("bias_mm")
        bias_done = signal("bias_done")
        x_io = signal("x_io")
        out_dma = signal("out_dma")
        pro_in = [signal(f"pro_in{i}") for i in range(ADA_RING)]
        pro_used = signal("pro_used", KT, ADA_RING)
        pro_sum = signal("pro_sum", 1)
        pro_read = signal("pro_read", 1, 1)

        class Layer:
            pass
        layers = []
        for l in range(DEPTH):
            s, n, first = Layer(), f"_{l}", l == 0
            s.raw_in = [signal(f"raw_in{i}" + n, HALF // NRAW * 16) for i in range(NRAW)]
            s.hi_done = signal("hi_done" + n, HALF)
            s.lo_done = signal("lo_done" + n, HALF, NRAW)
            s.mm_done = signal("mm_done" + n, HALF, NHL)
            more = 1 if first else 0
            full = [0, 0, SQ, SQ, 1, 10, 9, 1 + more]
            free = [6, 6, SQ, SQ, 2, 6, 5, 2 + more]
            s.full = [signal(f"full{b}" + n, full[b]) if full[b] else None for b in range(8)]
            s.free = [signal(f"free{b}" + n, free[b], 1) for b in range(8)]
            s.step_in = signal("step_in" + n, 160)
            s.pre, s.post = signal("dve_pre" + n), signal("dve_post" + n)
            s.own = signal("dve_own" + n, OWN_STEPS[l])
            s.act_own = signal("act_own" + n, 1)
            s.to_act = signal("to_act" + n, 4)
            s.from_act = signal("from_act" + n, 5)
            s.bb_done = signal("bb_done" + n, 1)
            s.xc_done = signal("xc_done" + n, 1)
            s.x_rot = signal("x_rot" + n, SQ)
            s.c_done = signal("c_done" + n, SQ, 1)
            s.p_norm = signal("p_norm" + n, 2)
            s.p_copy = signal("p_copy" + n, 8, 1)
            s.pv_done = signal("pv_done" + n, 8, 1)
            s.gate_used = [signal(f"gate_used{i}" + n, 2, 1) for i in range(2)]
            s.step_end = signal("step_end" + n, 1, 1)
            s.ada = KT * len(ADA_CHUNKS[l])
            s.ada_in = [signal(f"ada_in{i}" + n, s.ada // ADA_RING * 16) for i in range(ADA_RING)]
            s.ada_used = signal("ada_used" + n, s.ada, ADA_RING)
            s.from_one = [s.c_done, s.p_copy, s.pv_done, s.step_end, *s.gate_used, *s.free]
            s.h_bank = signal("h_bank" + n)
            s.hf_done = signal("hf_done" + n)
            s.op_hi = signal("op_hi_done" + n)
            s.op_lo = signal("op_lo_done" + n)
            s.glu_in = signal("glu_in" + n)
            s.glu_mm = signal("glu_mm" + n)
            s.glu_t = signal("glu_t" + n)
            s.diag = signal("diag" + n)
            s.gb_mm = signal("gb_mm" + n)
            s.gb = signal("gb" + n)
            s.z_in = signal("z_in" + n)
            s.y_mm = signal("y_mm" + n)
            s.y_used = signal("y_used" + n)
            s.d_done = signal("d_done" + n)
            s.var = signal("var" + n)
            s.std = signal("std" + n)
            s.xn = signal("xn" + n)
            layers.append(s)

        w_in_v = A["w_in"].rearrange("l (k p) n -> l p k n", p=P)
        w_out_v = A["w_out"].rearrange("l (k p) n -> l p k n", p=P)
        w_ada_v = A["w_ada"].rearrange("l (k p) n -> l k p n", p=P)
        x_v = A["x"].rearrange("b (s p) n -> p (b s) n", p=P)
        xn_v = x_norm.rearrange("(s p) n -> p s n", p=P)
        out_v = out.rearrange("b (s p) n -> p (b s) n", p=P)

        def unit_copied(eng, s, name, ct):
            u = UNITS.index(name)
            eng.wait_ge(s.free[u % 2].sem, s.free[u % 2].at(u // 2 + 1, ct))

        block = ctx.enter_context(nc.Block())

        @block.sync
        def _(sp):
            sp.dma_start(rel[:, :], A["rel_bias"].rearrange("b h -> h b"),
                         allow_slow_non_contiguous=True).then_inc(setup_dma.sem, 16)
            for l in range(DEPTH):
                if l:
                    sp.wait_ge(turned.sem, 4)
                for name, (at, n) in ROWS.items():
                    if name in ("s5_lam_re", "s5_lam_im"):
                        src = A[name][l].rearrange("(s g) p -> s (g p)", g=2)
                    elif name in ("conv_a", "conv_c"):
                        src = A[name][l].rearrange("k (t p) -> (k t) p", p=P)
                    else:
                        src = A[name][l].rearrange("(t p) -> t p", p=P)
                    sp.dma_start(rows[at:at + n, 0, :], src).then_inc(row_dma[l].sem, 16)
                sp.dma_start(rows[0:48, 1, :], A["b_ada"][l].rearrange("(t p) -> t p", p=P)).then_inc(row_dma[l].sem, 16)
                sp.dma_start(rows[48:64, 1, :], A["c"].rearrange("b (t p) -> (b t) p", p=P)).then_inc(row_dma[l].sem, 16)
                sp.dma_start(dt_in[:, :], A["s5_log_dt"][l].rearrange("(s g) -> s g", g=2)).then_inc(row_dma[l].sem, 16)
            sp.wait_ge(bias_row.sem, 1)
            sp.dma_start(bias_row_d, brow[:, 0, :]).then_inc(bias_io.sem, 16)
            sp.wait_ge(bias_io.sem, 16)
            for h in range(HEADS):
                src = bass.AP(tensor=bias_row_d.tensor, offset=bias_row_d[h, 0:1].offset, ap=[[1, P], [1, S]])
                sp.dma_start(work[:, h, :], src).then_inc(bias_io.sem, 16)
            with sp.Fori(0, 8) as chunk:
                for k in range(KT):
                    sp.wait_ge(pro_used.sem, chunk * KT + (k + 1))
                    sp.dma_start(ada_in[:, k % ADA_RING, :],
                                 w_ada_v[0, k, :, bass.ds(chunk * S, S)]).then_inc(pro_in[k % ADA_RING].sem, 16)
            sp.dma_start(z, x_v).then_inc(x_io.sem, 16)
            sp.wait_ge(bias_done.sem, HEADS)
            sp.dma_start(bias_d.rearrange("h p t -> p h t"), work[:, 8:16, :]).then_inc(bias_io.sem, 16)

            for l, s in enumerate(layers):
                if l == 0:
                    sp.wait_ge(pro_used.sem, pro_used.at(0, 8))
                else:
                    sp.wait_ge(layers[l - 1].lo_done.sem, layers[l - 1].lo_done.at(W_OUT, CT))
                with sp.Fori(0, CT) as ct:
                    for n in range(HALF):
                        at = ct * P + COLUMN[UNITS[n // 2]] * BR
                        if n != HALF - 2:
                            sp.wait_ge(s.lo_done.sem, ct * HALF + (n + 1 + (n == HALF - 3)))
                        sp.dma_start(raw[:, n % NRAW, :].rearrange("p (k n) -> p k n", k=KH),
                                     w_in_v[l, :, (n % 2) * KH:(n % 2 + 1) * KH,
                                            bass.ds(at, P)])\
                            .then_inc(s.raw_in[n % NRAW].sem, 16)
                        if n == NRAW - 1:
                            if l == 0:
                                sp.wait_ge(bias_io.sem, 16 * 10)
                            sp.wait_ge(s.step_end.sem, s.step_end.at(0, ct))
                            for i, name in enumerate(("s5_b_re", "s5_b_im")):
                                src = A[name][l].rearrange("(s g) p c -> (g p) s c", g=2)
                                sp.dma_start(s5_raw[:, i, :].rearrange("p (s c) -> p s c", s=SQ),
                                             src[:, bass.ds(ct * SQ, SQ), :]).then_inc(s.step_in.sem, 16)
                            for i, name in enumerate(("s5_c_re", "s5_c_im")):
                                src = A[name][l].rearrange("g c p -> (g c) p")
                                sp.dma_start(s5_raw[:, 2 + i, :], src[bass.ds(ct * P, P), :])\
                                    .then_inc(s.step_in.sem, 16)
                            for i, name in enumerate(("lru_wa", "lru_wx")):
                                src = A[name][l].rearrange("h i j -> (h i) j")
                                for h in range(2):
                                    sp.dma_start(lru_w[64 * h:64 * h + 64, i, 64 * h:64 * h + 64],
                                                 src[bass.ds(ct * P + 64 * h, 64), :]).then_inc(s.step_in.sem, 16)
                            for h in range(2):
                                sp.dma_start(bias_t[:, h, :],
                                             bias_d[bass.ds(ct * 2 + h, 1)].rearrange("o p t -> (o p) t"))\
                                    .then_inc(s.step_in.sem, 16)
                        if n >= NRAW:
                            for a in range(s.ada * (n - NRAW) // (HALF - NRAW), s.ada * (n + 1 - NRAW) // (HALF - NRAW)):
                                chunk, k = a // KT, a % KT
                                sp.wait_ge(s.ada_used.sem, ct * s.ada + (a + 1))
                                of, part = ADA_CHUNKS[l][chunk]
                                sp.dma_start(ada_in[:, a % ADA_RING, :],
                                             w_ada_v[of, k, :, bass.ds(ct * S + part * P, S)])\
                                    .then_inc(s.ada_in[a % ADA_RING].sem, 16)
                for n in range(W_OUT):
                    chunk, kk = n // 8, n % 8
                    sp.wait_ge(s.lo_done.sem, s.lo_done.at(n + 1 - NRAW, CT))
                    sp.dma_start(raw[:, n % NRAW, :].rearrange("p (k n) -> p k n", k=2),
                                 w_out_v[l, :, 2 * kk:2 * kk + 2, chunk * S:(chunk + 1) * S])\
                        .then_inc(s.raw_in[n % NRAW].sem, 16)
                    if n == NRAW - 1:
                        sp.wait_ge(s.step_end.sem, s.step_end.at(0, CT))
                        sp.dma_start(w_glu, A["s5_w_glu"][l].rearrange("(k p) n -> p k n", p=P))\
                            .then_inc(s.glu_in.sem, 16)
                    if n == 5:
                        sp.wait_ge(s.op_hi.sem, 2 * KT)
                        sp.wait_ge(s.op_lo.sem, 2 * KT)
                        sp.dma_start(z, x_v if l == 0 else xn_v).then_inc(s.z_in.sem, 16)
                        for i, name in ((0, "ln_g"), (1, "ln_b")):
                            if l:
                                sp.dma_start(ln_prev[:, i, :], A[name][l - 1].partition_broadcast(P))\
                                    .then_inc(s.z_in.sem, 16)
                            if l == DEPTH - 1:
                                sp.dma_start(ln_last[:, i, :], A[name][l].partition_broadcast(P))\
                                    .then_inc(s.z_in.sem, 16)
                if l < DEPTH - 1:
                    sp.wait_ge(s.xn.sem, ST)
                    sp.dma_start(xn_v, z).then_inc(x_io.sem, 16)
                    sp.wait_ge(x_io.sem, 32)
                else:
                    for t in range(ST):
                        sp.wait_ge(s.xn.sem, t + 1)
                        sp.dma_start(out_v[:, t, :], z[:, t, :]).then_inc(out_dma.sem, 16)
                    sp.wait_ge(out_dma.sem, 16 * ST)

        @block.gpsimd
        def _(pool):
            for sig in (pro_read, *layers[0].from_one, *layers[1].from_one):
                pool.sem_inc(sig.sem, 1)
            pool.memset(ident[:, :], 0.0).then_inc(const_done.sem, 1)
            pool.memset(flip[:, :], 0.0).then_inc(const_done.sem, 1)
            pool.memset(mask_row[:, :], 0.0).then_inc(const_done.sem, 1)
            pool.wait_ge(const_done.sem, 3)
            pool.affine_select(out=ident[:, :], in_=ident[:, :], compare_op=ALU.not_equal, fill=1.0, base=0,
                               pattern=[[-1, P]], channel_multiplier=1).then_inc(const_done.sem, 1)
            pool.affine_select(out=flip[:, :], in_=flip[:, :], compare_op=ALU.not_equal, fill=1.0, base=-(P - 1),
                               pattern=[[1, P]], channel_multiplier=1).then_inc(const_done.sem, 1)
            pool.memset(mask_row[:, :].rearrange("p (a b c) -> p a b c", b=2, c=CH)[:, :, 0, :], 1.0)\
                .then_inc(const_done.sem, 1)
            pool.iota(j_int[:, :], pattern=[[1, TC]], base=1, channel_multiplier=0).then_inc(const_done.sem, 1)
            pool.memset(ones[:, :], 1.0).then_inc(const_done.sem, 1)
            pool.memset(lru_w[:, :, :], 0.0).then_inc(const_done.sem, 1)
            pool.memset(xp[:, 0:3], 0.0).then_inc(const_done.sem, 1)
            pool.memset(va[:, 0:2], 0.0).then_inc(const_done.sem, 1)
            pool.memset(s5_bb[:, :, :, :, :], 0.0).then_inc(const_done.sem, 1)
            pool.memset(consts[:, 0:1], math.pi / 2).then_inc(const_done.sem, 1)
            pool.memset(consts[:, 1:2], EPS).then_inc(const_done.sem, 1)

            for l, s in enumerate(layers):
                pool.sem_inc(s.lo_done.sem, NRAW)
                for k in range(KT):
                    pool.wait_ge(s.op_hi.sem, k + 1)
                    pool.tensor_tensor(op_lo[:, k, :], hf[:, k % 2, :], op_hi[:, k, :].bitcast(F32),
                                       ALU.subtract).then_inc(s.op_lo.sem, 1)

                def split_lo(n, hi_at, mm_at):
                    pool.wait_ge(s.hi_done.sem, hi_at)
                    pool.wait_ge(s.mm_done.sem, mm_at)
                    pool.tensor_tensor(w_lo[:, n % NHL, :], raw[:, n % NRAW, :],
                                       w_hi[:, n % NHL, :].bitcast(F32), ALU.subtract).then_inc(s.lo_done.sem, 1)

                with pool.Fori(0, CT) as ct:
                    for n in range(HALF):
                        split_lo(n, s.hi_done.at(n + 1, ct), ct * HALF + (n + 1))
                for n in range(W_OUT):
                    split_lo(n, s.hi_done.at(n + 1, CT), W_LOOP + n + 1)

        @block.scalar
        def _(act):
            act.wait_ge(setup_dve.sem, 1)
            act.activation(cond[:, :], ada_b[:, 0, 48:64], ACT.Tanh, scale=0.5).then_inc(setup_act.sem, 1)
            for l in range(DEPTH):
                act.wait_ge(setup_dve.sem, 3 * l + 2)
                act.activation(dt_t[:, l, :], dt_t[:, l, :], ACT.Exp).then_inc(setup_act.sem, 1)
                act.wait_ge(setup_dve.sem, 3 * l + 3)
                act.activation(tmp[:, 2, 0:4], tmp[:, 2, 0:4], ACT.Exp).then_inc(setup_act.sem, 1)
                act.activation(tmp[:, 0, :], tmp[:, 0, :], ACT.Tanh, scale=0.5).then_inc(setup_act.sem, 1)
                act.activation(tmp[:, 5, :], tmp[:, 1, :], ACT.Sin, scale=TWO_PI).then_inc(setup_act.sem, 1)
                act.activation(tmp[:, 6, :], tmp[:, 1, :], ACT.Sin, scale=TWO_PI / 2).then_inc(setup_act.sem, 1)
                act.wait_ge(setup_dve.sem, 3 * l + 4)
                act.activation(tmp[:, 3, 0:4], tmp[:, 3, 0:4], ACT.Ln).then_inc(setup_act.sem, 1)
                act.wait_ge(setup_act.sem, 7 * l + 7)
                act.activation(tmp[:, 4, 0:4], tmp[:, 3, 0:4], ACT.Tanh, scale=0.5).then_inc(setup_act.sem, 1)
            for h in range(HEADS):
                act.wait_ge(bias_mm.sem, h + 1)
                act.activation(work[:, 8 + h, :], bank[h][:, :], ACT.Copy).then_inc(bias_done.sem, 1)

            for l, s in enumerate(layers):
                for k in range(KT):
                    act.wait_ge(s.hf_done.sem, k + 1)
                    act.activation(op_hi[:, k, :], hf[:, k % 2, :], ACT.Copy).then_inc(s.op_hi.sem, 1)

                def split_hi(n, step):
                    act.wait_ge(s.raw_in[n % NRAW].sem, s.raw_in[n % NRAW].at(16 * (n // NRAW + 1), step))
                    act.wait_ge(s.mm_done.sem, s.mm_done.at(n + 1 - NHL, step))
                    act.activation(w_hi[:, n % NHL, :], raw[:, n % NRAW, :], ACT.Copy).then_inc(s.hi_done.sem, 1)

                with act.Fori(0, CT) as ct:
                    def unit(name):
                        u = UNITS.index(name)
                        act.wait_ge(s.mm_done.sem, s.mm_done.at(2 * u + 2, ct))
                        return bank[u % 2][:, :], s.free[u % 2]

                    def copy(name, dst, scale=1.0):
                        ps, free = unit(name)
                        act.activation(dst, ps, ACT.Copy, scale=scale).then_inc(free.sem, 1)

                    def gate(name, i, use):
                        ps, free = unit(name)
                        act.wait_ge(s.gate_used[i].sem, s.gate_used[i].at(use, ct))
                        act.activation(gt[:, i, :], ps, ACT.Tanh, scale=0.5)
                        act.activation(gx[:, i, :], ps, ACT.Copy).then_inc(free.sem, 1)

                    def exps(h):
                        act.wait_ge(s.to_act.sem, s.to_act.at(2 + h, ct))
                        for t in range(ST):
                            pr = prob[:, P_AT[t]:P_AT[t] + P * (t + 1)]
                            e = act.activation(pr, pr, ACT.Exp, bias=soft[:, 1, t:t + 1], scale=1.0,
                                               accum_out=soft[:, 2, t:t + 1])
                        e.then_inc(s.from_act.sem, 1)

                    def p_copy(h, kb):
                        b, i = 5 + kb % 2, 4 * h + kb
                        use = 1 + 4 * h + 2 + kb // 2
                        act.wait_ge(s.full[b].sem, s.full[b].at(use + 1, ct))
                        act.wait_ge(s.pv_done.sem, s.pv_done.at(max(0, i - 1), ct))
                        act.activation(p_t[:, kb % 2, 0:P * (ST - kb)], bank[b][:, 0:P * (ST - kb)], ACT.Copy)\
                            .then_inc(s.p_copy.sem, 1)

                    def lru():
                        act.wait_ge(s.full[5].sem, s.full[5].at(1, ct))
                        act.wait_ge(s.full[6].sem, s.full[6].at(1, ct))
                        act.activation(lru_s[0], bank[5][:, :], ACT.Tanh, scale=0.5,
                                       bias=lru_c[:, l, bass.ds(ct + 4, 1)]).then_inc(s.free[5].sem, 1)
                        act.activation(lru_s[1], bank[6][:, :], ACT.Tanh, scale=0.5,
                                       bias=lru_c[:, l, bass.ds(ct + 8, 1)]).then_inc(s.free[6].sem, 1)
                        act.wait_ge(s.free[5].sem, s.free[5].at(1, ct))
                        act.activation(lru_s[0], lru_s[0], ACT.Tanh, scale=lru_c[:, l, bass.ds(ct, 1)],
                                       bias=lru_c[:, l, bass.ds(ct, 1)]).then_inc(s.act_own.sem, 1)
                        act.wait_ge(s.act_own.sem, s.act_own.at(1, ct))
                        act.activation(lru_s[2], lru_s[0], ACT.Sqrt).then_inc(s.from_act.sem, 1)

                    def rotation():
                        act.wait_ge(s.to_act.sem, s.to_act.at(1, ct))
                        act.activation(rot[:, 0, :, :], rot[:, 0, :, :], ACT.Sin, scale=TWO_PI)
                        act.activation(rot[:, 1, :, :], rot[:, 1, :, :], ACT.Sin, scale=-TWO_PI,
                                       bias=consts[:, 0:1]).then_inc(s.from_act.sem, 1)
                        act.wait_ge(s.full[4].sem, s.full[4].at(1, ct))
                        act.activation(s5_w[:, :, :].rearrange("p a b -> p (a b)"), bank[4][:, :], ACT.Copy)\
                            .then_inc(s.free[4].sem, 1)

                    for n in range(HALF):
                        split_hi(n, ct)
                        if n == 3:
                            act.wait_ge(s.free[4].sem, s.free[4].at(0, ct))
                            copy("d_u", u_d)
                        if n == 5:
                            act.wait_ge(s.step_end.sem, s.step_end.at(0, ct))
                            copy("c_x", xp[:, 3:3 + S])
                            rotation()
                        if n == 7:
                            copy("q", q_t, HD ** -0.5)
                        if n == 8:
                            lru()
                        if n == 9:
                            copy("k", k_t)
                        if n == 11:
                            copy("v", v_t)
                        if n == 13:
                            act.wait_ge(s.full[7].sem, s.full[7].at(s.full[7].per, ct))
                            act.wait_ge(s.pv_done.sem, s.pv_done.at(0, ct))
                            act.activation(work[:, 10, :], bank[7][:, :], ACT.Copy).then_inc(s.free[7].sem, 1)
                            exps(0)
                            gate("c_g", 0, 0)
                        if n == 15:
                            p_copy(0, 0)
                            p_copy(0, 1)
                            gate("d_g", 1, 0)
                        if n == 16:
                            p_copy(0, 2)
                            p_copy(0, 3)
                        if n == 17:
                            copy("a_c", va[:, 2:2 + S])
                        if n == 19:
                            copy("a_x", ax)
                        if n == 20:
                            exps(1)
                        if n == 21:
                            gate("b_g", 0, 1)
                        if n == 22:
                            p_copy(1, 0)
                            p_copy(1, 1)
                        if n == 23:
                            p_copy(1, 2)
                            p_copy(1, 3)
                            gate("a_g", 1, 1)
                            act.wait_ge(s.to_act.sem, s.to_act.at(4, ct))
                            act.activation(gel, gel, ACT.Tanh, scale=GELU_C).then_inc(s.from_act.sem, 1)

                split_hi(0, CT)
                split_hi(1, CT)
                act.wait_ge(s.mm_done.sem, s.mm_done.at(0, CT))
                act.wait_ge(s.step_end.sem, s.step_end.at(0, CT))
                for k in range(12):
                    act.activation(op_hi[:, k, :], y_t[:, k, :], ACT.Copy).then_inc(s.op_hi.sem, 1)
                for m in range(4):
                    act.wait_ge(s.glu_mm.sem, m + 1)
                    act.activation(glu_t[:, m, :], bank[4 + m][:, :], ACT.Tanh, scale=0.5,
                                   bias=glu_hb[:, l, m:m + 1]).then_inc(s.glu_t.sem, 1)
                for c in range(4):
                    act.wait_ge(s.gb_mm.sem, c + 1)
                    act.activation(gate_b[:, c, :], bank[4 + c][:, :], ACT.Copy).then_inc(s.gb.sem, 1)
                for m in range(4):
                    act.wait_ge(s.d_done.sem, m + 1)
                    act.activation(op_hi[:, 12 + m, :], y_t[:, 12 + m, :], ACT.Copy).then_inc(s.op_hi.sem, 1)
                for n in range(2, W_OUT):
                    split_hi(n, CT)
                for t in range(ST):
                    act.wait_ge(s.var.sem, t + 1)
                    act.activation(mv[:, t, 2:3], mv[:, t, 1:2], ACT.Sqrt, bias=consts[:, 1:2], scale=1.0)\
                        .then_inc(s.std.sem, 1)

        @block.tensor
        def _(pe):
            def turn(out_, in_, sig):
                n = in_.shape[0]
                return pe.transpose(out_, in_, ident[0:n, 0:n]).then_inc(sig.sem, 1)

            pe.wait_ge(const_done.sem, 14)
            for l in range(DEPTH):
                pe.wait_ge(row_dma[l].sem, 16 * 15)
                b = 4 * l
                turn(bank[b][:, 0:N_ROWS], rows[0:N_ROWS, 0, :], turned)
                turn(bank[b + 1][:, 0:64], rows[0:64, 1, :], turned)
                pe.wait_ge(setup_own.sem, l + 1)
                turn(bank[b + 2][:, 0:16], dt_row[:, :], turned)
                if l == 0:
                    turn(bank[3][:, 0:32], mask_row[:, :], turned)
            pe.wait_ge(setup_dve.sem, 5)
            pe.wait_ge(bias_io.sem, 16 * 9)
            for h in range(HEADS):
                pe.matmul(bank[h][:, :], flip[:, :], work[:, h, :], start=True, stop=True).then_inc(bias_mm.sem, 1)
            pe.wait_ge(bias_done.sem, HEADS)
            with pe.Fori(0, 8) as chunk:
                pe.wait_ge(pro_used.sem, pro_used.at(KT, chunk))
                pe.wait_ge(pro_read.sem, pro_read.at(0, chunk))
                for j in range(4):
                    mm = pe.matmul(bank[0][:, j:j + 1], ada_acc[:, 0, P * j:P * (j + 1)], ones[:, 0:1],
                                   start=True, stop=True)
                mm.then_inc(pro_sum.sem, 1)

            for l, s in enumerate(layers):
                pe.sem_inc(s.mm_done.sem, NHL)
                if l == 0:
                    pe.wait_ge(x_io.sem, 16)
                    pe.wait_ge(pro_read.sem, 9)
                else:
                    pe.wait_ge(layers[l - 1].xn.sem, ST)
                for k in range(KT):
                    if k >= 4:
                        pe.wait_ge(s.hf_done.sem, k - 3)
                    for t in range(ST):
                        mm = pe.transpose(bank[k % 4][:, P * t:P * (t + 1)], z[:, t, P * k:P * (k + 1)], ident[:, :])
                    mm.then_inc(s.h_bank.sem, 1)
                pe.wait_ge(s.hf_done.sem, KT)

                def product(out_, xs, ws, first, last):
                    (xh, xl), (wh, wl) = xs, ws
                    pe.matmul(out_, xh, wh, start=first, stop=False)
                    pe.matmul(out_, xh, wl, start=False, stop=False)
                    return pe.matmul(out_, xl, wh, start=False, stop=last)

                with pe.Fori(0, CT) as ct:
                    def is_free(b, use):
                        pe.wait_ge(s.free[b].sem, s.free[b].at(use, ct))

                    def fill(b, mm):
                        mm.then_inc(s.full[b].sem, 1)

                    def s5_turn():
                        pe.wait_ge(s.bb_done.sem, s.bb_done.at(1, ct))
                        is_free(4, 0)
                        for i in range(2):
                            pe.transpose(bank[4][:, P * i:P * (i + 1)],
                                         s5_bb[:, i, :, :, :].rearrange("p a b c -> p (a b c)"), ident[:, :])
                        for i in range(2):
                            mm = pe.transpose(bank[4][:, P * (2 + i):P * (3 + i)],
                                              s5_cc[:, i, :, :].rearrange("p a b -> p (a b)"), ident[:, :])
                        fill(4, mm)

                    def s5_drive(q):
                        if q == 0:
                            unit_copied(pe, s, "d_u", ct)
                            is_free(4, 1)
                        for i in range(2):
                            is_free(2 + i, q)
                            fill(2 + i, pe.matmul(bank[2 + i][:, :], s5_w[32 * q:32 * q + 32, i, :],
                                                  u_d[32 * q:32 * q + 32, :], start=True, stop=True))

                    def s5_output(q):
                        pe.wait_ge(s.x_rot.sem, s.x_rot.at(q + 1, ct))
                        o = bank[4][32 * q:32 * q + 32, :]
                        pe.matmul(o, s5_w[:, 2, 32 * q:32 * q + 32], s5_s[3], start=True, stop=False)
                        mm = pe.matmul(o, s5_w[:, 3, 32 * q:32 * q + 32], s5_s[4], start=False, stop=True)
                        mm.then_inc(s.c_done.sem, 1)

                    def lru_gates():
                        pe.wait_ge(s.xc_done.sem, s.xc_done.at(1, ct))
                        pe.wait_ge(s.step_in.sem, s.step_in.at(160, ct))
                        pe.wait_ge(s.p_copy.sem, s.p_copy.at(0, ct))
                        for i in range(2):
                            is_free(5 + i, 0)
                            fill(5 + i, pe.matmul(bank[5 + i][:, :], lru_w[:, i, :], xc, start=True, stop=True))

                    def scores(h, t):
                        b = 5 + t % 2
                        if h == 0 and t == 0:
                            unit_copied(pe, s, "q", ct)
                            unit_copied(pe, s, "k", ct)
                            pe.wait_ge(s.step_in.sem, s.step_in.at(160, ct))
                        if h == 1:
                            pe.wait_ge(s.p_copy.sem, s.p_copy.at(ST, ct))
                        is_free(b, 1 + 2 * h + t // 2)
                        fill(b, pe.matmul(bank[b][:, 0:P * (t + 1)], q_t[64 * h:64 * h + 64, P * t:P * (t + 1)],
                                          k_t[64 * h:64 * h + 64, 0:P * (t + 1)], start=True, stop=True))

                    def p_turn(h, kb):
                        b = 5 + kb % 2
                        pe.wait_ge(s.p_norm.sem, s.p_norm.at(h + 1, ct))
                        if kb >= 2:
                            pe.wait_ge(s.p_copy.sem, s.p_copy.at(ST * h + kb - 1, ct))
                        for t in range(kb, ST):
                            mm = pe.transpose(bank[b][:, P * (t - kb):P * (t - kb + 1)],
                                              prob[:, P_AT[t] + P * kb:P_AT[t] + P * (kb + 1)], ident[:, :])
                        fill(b, mm)

                    def weigh(h, kb):
                        pe.wait_ge(s.p_copy.sem, s.p_copy.at(4 * h + kb + 1, ct))
                        if h == 0 and kb == 0:
                            is_free(7, s.free[7].per - 1)
                        pe.matmul(bank[7][64 * h:64 * h + 64, P * kb:S], v_s[:, kb, 64 * h:64 * h + 64],
                                  p_t[:, kb % 2, 0:P * (ST - kb)], start=kb == 0, stop=kb == ST - 1)\
                            .then_inc(s.pv_done.sem, 1)

                    def v_turn():
                        unit_copied(pe, s, "v", ct)
                        is_free(7, s.free[7].per - 2)
                        for t in range(ST):
                            mm = pe.transpose(bank[7][:, P * t:P * (t + 1)], v_t[:, P * t:P * (t + 1)], ident[:, :])
                        fill(7, mm)

                    def ada_sum(last):
                        b, use = (5, 5) if last else (7, 0)
                        pe.wait_ge(s.ada_used.sem, s.ada_used.at(s.ada if last else KT, ct))
                        if last:
                            pe.wait_ge(s.p_copy.sem, s.p_copy.at(2 * ST, ct))
                        is_free(b, use)
                        for i, chunk in enumerate(ada_group(l, last)):
                            for j in range(4):
                                mm = pe.matmul(bank[b][:, 4 * i + j:4 * i + j + 1],
                                               ada_acc[:, chunk % 2, P * j:P * (j + 1)], ones[:, 0:1],
                                               start=True, stop=True)
                        fill(b, mm)

                    between = [[] for _ in range(HALF)]

                    def put(n, part, *args):
                        between[n].append(lambda: part(*args))

                    put(3, s5_turn)
                    put(6, lru_gates)
                    for q, (at_drive, at_output) in enumerate(((5, 9), (7, 12), (10, 16), (13, 19))):
                        put(at_drive, s5_drive, q)
                        put(at_output, s5_output, q)
                    if l == 0:
                        put(10, ada_sum, False)
                    for h, at in ((0, 10), (1, 16)):
                        for t in range(ST):
                            put(at + t // 2 * (1 + h), scores, h, t)
                    put(11, v_turn)
                    for h, at in ((0, 13), (1, 20)):
                        put(at, p_turn, h, 0)
                        put(at, p_turn, h, 1)
                        put(at + 1, weigh, h, 0)
                        put(at + 1, weigh, h, 1)
                        put(at + 1, p_turn, h, 2)
                        put(at + 1, p_turn, h, 3)
                        put(at + 2, weigh, h, 2)
                        put(at + 2, weigh, h, 3)
                    put(HALF - 1, ada_sum, True)

                    for n in range(HALF):
                        u, half = n // 2, n % 2
                        if half == 0:
                            is_free(u % 2, u // 2)
                        pe.wait_ge(s.lo_done.sem, s.lo_done.at(n + 1, ct))
                        for j in range(KH):
                            k = half * KH + j
                            if u == 0:
                                pe.wait_ge(s.op_lo.sem, k + 1)
                            w = slice(P * j, P * (j + 1))
                            mm = product(bank[u % 2][:, :], (w_hi[:, n % NHL, w], w_lo[:, n % NHL, w]),
                                         (op_hi[:, k, :], op_lo[:, k, :]), k == 0, k == KT - 1)
                        mm.then_inc(s.mm_done.sem, 1)
                        for part in between[n]:
                            part()

                pe.wait_ge(s.glu_in.sem, 16)
                pe.wait_ge(s.step_end.sem, s.step_end.at(0, CT))
                for m in range(4):
                    for k in range(4):
                        mm = pe.matmul(bank[4 + m][:, :], w_glu[:, k, P * m:P * (m + 1)], y_t[:, 12 + k, :],
                                       start=k == 0, stop=k == 3)
                    mm.then_inc(s.glu_mm.sem, 1)
                for c in range(4):
                    pe.wait_ge(s.diag.sem, c + 1)
                    pe.wait_ge(s.glu_t.sem, c + 1)
                    pe.matmul(bank[4 + c][:, :], ones[:, :], diag[:, c % 2, :], start=True, stop=True)\
                        .then_inc(s.gb_mm.sem, 1)
                for b in range(4):
                    pe.wait_ge(s.free[b].sem, s.free[b].at(0, CT))
                for n in range(W_OUT):
                    c, kk = n // 8, n % 8
                    if n == 8:
                        pe.wait_ge(s.gb.sem, 4)
                    pe.wait_ge(s.lo_done.sem, s.lo_done.at(n + 1, CT))
                    for t in range(ST):
                        if c >= 2 and kk == 0:
                            pe.wait_ge(s.y_used.sem, 4 * (c - 2) + t + 1)
                        for j in range(2):
                            k = 2 * kk + j
                            if c == 0 and t == 0:
                                pe.wait_ge(s.op_lo.sem, KT + k + 1)
                            x_, w_ = slice(P * t, P * (t + 1)), slice(S * j, S * (j + 1))
                            mm = product(bank[4 * (c % 2) + t][:, :], (op_hi[:, k, x_], op_lo[:, k, x_]),
                                         (w_hi[:, n % NHL, w_], w_lo[:, n % NHL, w_]), k == 0, k == KT - 1)
                        if kk == 7 and t < ST - 1:
                            mm.then_inc(s.y_mm.sem, 1)
                    mm.then_inc(s.mm_done.sem, 1)

        def branch_loop(dve, l, s, line, own, tt, ts, stt, repeat):
            ADD, SUB, MUL = ALU.add, ALU.subtract, ALU.mult
            pr = {name: at for name, (at, _) in ROWS.items()}
            with dve.Fori(0, CT) as ct:
                counted = [s.own, s.to_act, s.p_norm, s.x_rot, s.xc_done, s.bb_done, s.step_end,
                           *s.gate_used, *s.free, s.ada_used]
                line.enter(ct, *counted)
                for b, before in ((1, 5), (4, 1), (5, 1), (6, 1), (7, s.free[7].per - 1)):
                    s.free[b].local = before
                pieces = [0]

                def ada(count):
                    for _ in range(count if l == 0 else min(1, s.ada - pieces[0])):
                        a = pieces[0]
                        pieces[0] += 1
                        chunk, k = a // KT, a % KT
                        acc, src = ada_acc[:, chunk % 2, :], ada_in[:, a % ADA_RING, :]
                        dve.wait_ge(s.ada_in[a % ADA_RING].sem, s.ada_in[a % ADA_RING].at(16 * (a // ADA_RING + 1), ct))
                        if k:
                            dve.wait_ge(s.ada_used.sem, s.ada_used.at(a, ct))
                            stt(acc, src, cond[:, k:k + 1], acc, MUL, ADD).then_inc(s.ada_used.sem, 1)
                        else:
                            ts(acc, src, cond[:, 0:1], MUL).then_inc(s.ada_used.sem, 1)

                def ada_read(last):
                    b, use = (5, 10) if last else (7, 1)
                    dve.wait_ge(s.full[b].sem, s.full[b].at(use, ct))
                    group = ada_group(l, last)
                    for i, chunk in enumerate(group):
                        of, part = ADA_CHUNKS[l][chunk]
                        to = bass.ds(ct * 4 + part, 4)
                        read = tt(ada_t[:, of, to], bank[b][:, 4 * i:4 * i + 4], ada_b[:, of, to], ADD)
                        if i == len(group) - 1:
                            read.then_inc(s.free[b].sem, 1)
                        else:
                            own(read, s.own)

                def col(name, k=0):
                    return par[:, l, bass.ds(ct + (pr[name] + k), 1)]

                def y_out(branch):
                    return y_t[:, bass.ds(ct + 4 * branch, 1), :].rearrange("p o t -> p (o t)")

                dve.wait_ge(s.step_in.sem, s.step_in.at(160, ct))
                own(dve.tensor_copy(s5_k[:, :, :], s5c[:, l, :, bass.ds(ct * SQ, SQ)]), s.own)
                turns = rot[:, 0, :, :]
                j_all = j_row[:, :].unsqueeze(1).to_broadcast([P, SQ, TC])
                own(tt(turns, repeat(s5_k[:, 1, :], TC), j_all, MUL), s.own)
                own(ts(rot[:, 1, :, :], turns, ROUND, ADD, ROUND, SUB), s.own)
                own(tt(turns, turns, rot[:, 1, :, :], SUB), s.own)
                own(stt(rot[:, 1, :, :], turns, -1.0, turns, MUL, ALU.max), s.to_act)
                for i in range(2):
                    for g in range(2):
                        c_in = s5_raw[:, 2 + i, :]
                        own(ts(s5_cc[:, i, g, :], c_in, mask[:, 2 * i + g:2 * i + g + 1], MUL), s.own)
                t1 = s5_s[2][:, 0:64].rearrange("p (s c) -> p s c", s=SQ)
                t2 = s5_s[2][:, 64:128].rearrange("p (s c) -> p s c", s=SQ)
                b_re, b_im = (s5_raw[:, i, :].rearrange("p (s c) -> p s c", s=SQ) for i in range(2))
                f_re, f_im = repeat(s5_k[:, 2, :], CH), repeat(s5_k[:, 3, :], CH)
                for i, (u_, v_, op) in enumerate(((b_re, b_im, SUB), (b_im, b_re, ADD))):
                    own(tt(t1, u_, f_re, MUL), s.own)
                    own(tt(t2, v_, f_im, MUL), s.own)
                    for g in range(2):
                        h = slice(64 * g, 64 * g + 64)
                        o = s5_bb[h, i, :, g, :]
                        op_ = tt(o, t1[h], t2[h], op)
                        if i == 1 and g == 1:
                            own(op_, s.bb_done)
                        else:
                            own(op_, s.own)
                ada(4)

                unit_copied(dve, s, "c_x", ct)
                own(ts(xc, xp[:, 3:3 + S], col("conv_c", 12), MUL, col("conv_c_b"), ADD), s.own)
                for k in (2, 1):
                    own(stt(xc, xp[:, k:k + S], col("conv_c", 4 * k), xc, MUL, ADD), s.own)
                own(stt(xc, xp[:, 0:S], col("conv_c"), xc, MUL, ADD), s.xc_done)
                ada(4)

                def s5_tile(q):
                    cos = rot[:, 1, q, :].unsqueeze(1).to_broadcast([P, 4, TC])
                    sin = rot[:, 0, q, :].unsqueeze(1).to_broadcast([P, 4, TC])
                    w_re, w_im, t_, x_re, x_im = (v.rearrange("p (a b) -> p a b", a=4) for v in s5_s)
                    if q == 0:
                        dve.wait_ge(s.from_act.sem, s.from_act.at(1, ct))
                    dve.wait_ge(s.full[2].sem, s.full[2].at(q + 1, ct))
                    dve.wait_ge(s.full[3].sem, s.full[3].at(q + 1, ct))
                    bu_re, bu_im = (bank[2 + i][:, :].rearrange("p (a b) -> p a b", a=4) for i in range(2))
                    own(tt(w_re, bu_re, cos, MUL), s.own)
                    own(tt(t_, bu_im, sin, MUL), s.own)
                    own(tt(w_re, w_re, t_, ADD), s.own)
                    own(tt(w_im, bu_im, cos, MUL), s.free[3])
                    own(tt(t_, bu_re, sin, MUL), s.free[2])
                    own(tt(w_im, w_im, t_, SUB), s.own)
                    mag = s5_k[:, 0, q:q + 1].to_broadcast([P, TC])
                    cl, sl = rot[:, 1, q, TC - 1:TC], rot[:, 0, q, TC - 1:TC]
                    for c in range(S // TC):
                        i_re, i_im = (0.0, 0.0) if c == 0 else (carry[:, 1:2], carry[:, 3:4])
                        a, b = (v[:, c * TC:(c + 1) * TC] for v in s5_s[0:2])
                        own(dve.tensor_tensor_scan(a, mag, a, i_re, MUL, ADD), s.own)
                        own(dve.tensor_tensor_scan(b, mag, b, i_im, MUL, ADD), s.own)
                        if c < S // TC - 1:
                            e_re, e_im = a[:, TC - 1:TC], b[:, TC - 1:TC]
                            own(tt(carry[:, 0:1], e_im, sl, MUL), s.own)
                            own(tt(carry[:, 2:3], e_im, cl, MUL), s.own)
                            own(stt(carry[:, 1:2], e_re, cl, carry[:, 0:1], MUL, SUB), s.own)
                            own(stt(carry[:, 3:4], e_re, sl, carry[:, 2:3], MUL, ADD), s.own)
                    ada(2)
                    dve.wait_ge(s.c_done.sem, s.c_done.at(q, ct))
                    own(tt(x_re, w_re, cos, MUL), s.own)
                    own(tt(t_, w_im, sin, MUL), s.own)
                    own(tt(x_re, x_re, t_, SUB), s.own)
                    own(tt(x_im, w_im, cos, MUL), s.own)
                    own(tt(t_, w_re, sin, MUL), s.own)
                    own(tt(x_im, x_im, t_, ADD), s.x_rot)

                def score_max(h, ts_):
                    for t in ts_:
                        b, use = 5 + t % 2, 1 + 4 * h + t // 2
                        w = P * (t + 1)
                        dve.wait_ge(s.full[b].sem, s.full[b].at(use + 1, ct))
                        line(dve.memset(spare[:, :], 0.0), s.own)
                        own(dve.tensor_tensor_reduce(prob[:, P_AT[t]:P_AT[t] + w], bank[b][:, 0:w],
                                                      bias_t[:, h, S - w:S], 1.0, -3e38, ADD, ALU.max,
                                                      soft[:, 0, t:t + 1]), s.free[b])
                    if ts_[-1] == 3:
                        own(ts(soft[:, 1, :], soft[:, 0, :], -1.0, MUL), s.to_act)

                def normalise(h):
                    dve.wait_ge(s.from_act.sem, s.from_act.at(3 + h, ct))
                    own(dve.reciprocal(soft[:, 3, :], soft[:, 2, :]), s.own)
                    for t in range(ST):
                        pt = prob[:, P_AT[t]:P_AT[t] + P * (t + 1)]
                        own(ts(pt, pt, soft[:, 3, t:t + 1], MUL), s.own if t < 3 else s.p_norm)

                def silu2(i, use_name, dst):
                    unit_copied(dve, s, use_name, ct)
                    return stt(dst, gt[:, i, :], 1.0, gx[:, i, :], ADD, MUL)

                s5_tile(0)
                ada(2)
                dve.wait_ge(s.from_act.sem, s.from_act.at(2, ct))
                own(ts(lru_s[0], lru_s[0], 1.0, ADD), s.own)
                own(dve.reciprocal(lru_s[0], lru_s[0]), s.own)
                own(tt(lru_s[2], lru_s[2], lru_s[0], MUL), s.own)
                own(ts(lru_s[0], lru_s[0], 2.0, MUL, -1.0, ADD), s.own)
                own(stt(lru_s[1], lru_s[1], 1.0, xc, ADD, MUL), s.own)
                own(tt(lru_s[1], lru_s[1], lru_s[2], MUL), s.own)
                own(dve.tensor_tensor_scan(xc, lru_s[0], lru_s[1], 0.0, MUL, ADD), s.own)
                ada(2)
                s5_tile(1)
                ada(2)
                if l == 0:
                    ada_read(False)
                score_max(0, (0, 1))
                ada(2)
                score_max(0, (2, 3))
                ada(3)
                normalise(0)
                s5_tile(2)
                own(silu2(0, "c_g", gx[:, 0, :]), s.own)
                dve.wait_ge(x_io.sem, 16 * (l + 1))
                own(stt(y_out(2), xc, 0.5, gx[:, 0, :], MUL, MUL), s.gate_used[0])
                ada(2)
                s5_tile(3)
                ada(2)
                score_max(1, (0, 1))
                ada(3)
                score_max(1, (2, 3))
                own(silu2(1, "d_g", silu_d[:, bass.ds(ct, 1), :].rearrange("p o t -> p (o t)")), s.gate_used[1])
                ada(3)
                normalise(1)
                y = s5_s[0]
                dve.wait_ge(s.c_done.sem, s.c_done.at(SQ, ct))
                own(stt(y, u_d, col("s5_d"), bank[4][:, :], MUL, ADD), s.free[4])
                own(tt(s5_s[2], y, y, MUL), s.own)
                own(ts(s5_s[2], s5_s[2], 0.044715, MUL, 1.0, ADD), s.own)
                own(tt(gel, s5_s[2], y, MUL), s.to_act)
                ada(3)
                unit_copied(dve, s, "a_x", ct)
                v = va[:, 2:2 + S]
                own(tt(v, v, ax, MUL), s.own)
                cv = s5_s[1]
                own(ts(cv, v, col("conv_a", 8), MUL), s.own)
                own(stt(cv, va[:, 1:1 + S], col("conv_a", 4), cv, MUL, ADD), s.own)
                own(stt(cv, va[:, 0:S], col("conv_a"), cv, MUL, ADD), s.own)
                ada(4)
                own(silu2(0, "b_g", gx[:, 0, :]), s.own)
                dve.wait_ge(s.pv_done.sem, s.pv_done.at(2 * ST, ct))
                own(stt(s5_s[2], bank[7][:, :], 0.5, gx[:, 0, :], MUL, MUL), s.free[7])
                own(dve.tensor_copy(y_out(1), s5_s[2]), s.gate_used[0])
                ada(4)
                own(silu2(1, "a_g", gx[:, 1, :]), s.own)
                dve.wait_ge(s.mm_done.sem, s.mm_done.at(HALF, ct))
                own(tt(cv, cv, bank[1][:, :], MUL), s.free[1])
                own(stt(y_out(0), cv, 0.5, gx[:, 1, :], MUL, MUL), s.gate_used[1])
                ada_read(True)
                dve.wait_ge(s.from_act.sem, s.from_act.at(5, ct))
                own(stt(y, gel, 1.0, y, ADD, MUL), s.own)
                own(ts(y_out(3), y, 0.5, MUL), s.step_end)
                assert s.own.local == s.own.per, s.own.local
                assert pieces[0] == s.ada, pieces[0]
                for sig in counted:
                    sig.local = 0
                line.step = CT
            line.last = None

        @block.vector
        def _(dve):
            line = Line(dve)

            def own(ins, sig):
                line(ins, sig)
                line.settle()

            def tt(o, a, b, op):
                return dve.tensor_tensor(o, a, b, op)

            def ts(o, a, s1, op0, s2=None, op1=None):
                if op1 is None:
                    return dve.tensor_scalar(o, a, s1, None, op0)
                return dve.tensor_scalar(o, a, s1, s2, op0, op1)

            def stt(o, a, sc, b, op0, op1):
                return dve.scalar_tensor_tensor(o, a, sc, b, op0, op1)

            def repeat(col, n):
                return col.unsqueeze(2).to_broadcast([col.shape[0], col.shape[1], n])

            ADD, SUB, MUL = ALU.add, ALU.subtract, ALU.mult
            chain = Signal(setup_own.sem, 0, 0)
            steps = Signal(setup_dve.sem, 0, 0)

            dve.wait_ge(const_done.sem, 14)
            dve.sem_inc(pro_used.sem, ADA_RING)
            for s in layers:
                dve.sem_inc(s.ada_used.sem, ADA_RING)
            sched = Signal(bias_own.sem, 0, 0)
            dve.wait_ge(setup_dma.sem, 16)
            last = S - 1
            near = last - P
            own(dve.memset(brow[:, :, :], NEG), sched)
            own(dve.memset(brow[:, 1, 3:S:4], 0.0), sched)
            own(dve.memset(brow[:, 1, 15:S:16], math.log(2)), sched)
            own(dve.memset(brow[:, 1, near:S], 0.0), sched)
            own(dve.memset(brow[:, 1, near:S:4], math.log(2)), sched)
            own(dve.memset(brow[:, 1, near:S:16], math.log(3)), sched)
            d = 0
            while d < S:
                e = d
                while e + 1 < S and bucket_of(e + 1) == bucket_of(d):
                    e += 1
                k = bucket_of(d)
                own(dve.tensor_copy(brow[:, 0, last - e:last - d + 1],
                                    rel[:, k:k + 1].to_broadcast([HEADS, e - d + 1])), sched)
                d = e + 1
            tt(brow[:, 0, 0:S], brow[:, 0, 0:S], brow[:, 1, 0:S], ADD).then_inc(bias_row.sem, 1)

            own(dve.tensor_copy(j_row[:, :], j_int[:, :]), sched)
            for l in range(DEPTH):
                dve.wait_ge(row_dma[l].sem, 16 * 15)
                line(dve.tensor_copy(dt_row[:, :].rearrange("s (g p) -> s g p", g=2), repeat(dt_in[:, :], NS)), chain)
                b = 4 * l
                dve.wait_ge(turned.sem, 3 + 4 * l if l else 4)
                own(dve.tensor_copy(par[:, l, :], bank[b][:, 0:N_ROWS]), sched)
                own(dve.tensor_copy(ada_b[:, l, :], bank[b + 1][:, 0:64]), sched)
                if l == 0:
                    own(dve.tensor_copy(mask[:, 0:1], bank[3][:, 0:1]), sched)
                    own(ts(mask[:, 1:2], mask[:, 0:1], -1.0, MUL, 1.0, ADD), sched)
                    own(ts(mask[:, 2:4], mask[:, 0:2], -1.0, MUL), sched)
                    line(dve.tensor_copy(gate1[:, :], ada_b[:, 0, 48:64]), steps)
                    dve.wait_ge(setup_act.sem, 1)
                    line.settle()
                    own(stt(cond[:, :], cond[:, :], 1.0, gate1[:, :], ADD, MUL), sched)
                    own(ts(cond[:, :], cond[:, :], 0.5, MUL), sched)
                line(dve.tensor_copy(dt_t[:, l, :], bank[b + 2][:, 0:16]), steps)
                dve.wait_ge(setup_act.sem, 7 * l + 2)
                lam = ROWS["s5_lam_re"][0]
                re, im, dt = par[:, l, lam:lam + 16], par[:, l, lam + 16:lam + 32], dt_t[:, l, :]
                lru = ROWS["lru_lambda"][0]
                lrl = par[:, l, lru:lru + 4]
                own(tt(tmp[:, 0, :], re, dt, MUL), sched)
                own(tt(tmp[:, 1, :], im, dt, MUL), sched)
                own(ts(tmp[:, 1, :], tmp[:, 1, :], 1 / (2 * math.pi), MUL), sched)
                own(ts(tmp[:, 7, :], tmp[:, 1, :], ROUND, ADD, ROUND, SUB), sched)
                own(tt(tmp[:, 1, :], tmp[:, 1, :], tmp[:, 7, :], SUB), sched)
                own(dve.tensor_copy(s5c[:, l, 1, :], tmp[:, 1, :]), sched)
                own(ts(tmp[:, 2, 0:4], lrl, -1.0, MUL), sched)
                own(ts(tmp[:, 2, 4:8], tmp[:, 2, 0:4], 0.0, ALU.max), sched)
                own(tt(tmp[:, 2, 8:12], tmp[:, 2, 0:4], lrl, ALU.min), sched)
                line(dve.tensor_copy(tmp[:, 2, 0:4], tmp[:, 2, 8:12]), steps)
                dve.wait_ge(setup_act.sem, 7 * l + 6)
                line(ts(tmp[:, 3, 0:4], tmp[:, 2, 0:4], 1.0, ADD), steps)
                own(ts(tmp[:, 7, :], tmp[:, 0, :], -1.0, MUL, 1.0, ADD), sched)
                own(dve.reciprocal(tmp[:, 7, :], tmp[:, 7, :]), sched)
                own(stt(tmp[:, 0, :], tmp[:, 0, :], 2.0, tmp[:, 7, :], MUL, MUL), sched)
                own(ts(s5c[:, l, 0, :], tmp[:, 0, :], 1.0, ADD), sched)
                own(tt(tmp[:, 6, :], tmp[:, 6, :], tmp[:, 6, :], MUL), sched)
                own(stt(tmp[:, 6, :], tmp[:, 6, :], -2.0, s5c[:, l, 0, :], MUL, MUL), sched)
                own(tt(tmp[:, 0, :], tmp[:, 0, :], tmp[:, 6, :], ADD), sched)
                own(tt(tmp[:, 5, :], tmp[:, 5, :], s5c[:, l, 0, :], MUL), sched)
                own(tt(tmp[:, 6, :], re, re, MUL), sched)
                own(tt(tmp[:, 7, :], im, im, MUL), sched)
                own(tt(tmp[:, 7, :], tmp[:, 7, :], tmp[:, 6, :], ADD), sched)
                own(dve.reciprocal(tmp[:, 7, :], tmp[:, 7, :]), sched)
                own(tt(tmp[:, 6, :], tmp[:, 0, :], re, MUL), sched)
                own(tt(tmp[:, 1, :], tmp[:, 5, :], im, MUL), sched)
                own(tt(tmp[:, 6, :], tmp[:, 6, :], tmp[:, 1, :], ADD), sched)
                own(tt(s5c[:, l, 2, :], tmp[:, 6, :], tmp[:, 7, :], MUL), sched)
                own(tt(tmp[:, 6, :], tmp[:, 5, :], re, MUL), sched)
                own(tt(tmp[:, 1, :], tmp[:, 0, :], im, MUL), sched)
                own(tt(tmp[:, 6, :], tmp[:, 6, :], tmp[:, 1, :], SUB), sched)
                own(tt(s5c[:, l, 3, :], tmp[:, 6, :], tmp[:, 7, :], MUL), sched)
                dve.wait_ge(setup_act.sem, 7 * l + 8)
                own(ts(tmp[:, 4, 4:8], tmp[:, 4, 0:4], -1.0, MUL, 1.0, ADD), sched)
                own(dve.reciprocal(tmp[:, 4, 4:8], tmp[:, 4, 4:8]), sched)
                own(stt(tmp[:, 4, 0:4], tmp[:, 4, 0:4], 2.0, tmp[:, 4, 4:8], MUL, MUL), sched)
                own(tt(tmp[:, 4, 4:8], tmp[:, 2, 0:4], tmp[:, 4, 0:4], SUB), sched)
                own(ts(tmp[:, 4, 0:4], tmp[:, 4, 0:4], 1.0, ADD), sched)
                own(dve.reciprocal(tmp[:, 4, 0:4], tmp[:, 4, 0:4]), sched)
                own(tt(tmp[:, 4, 4:8], tmp[:, 4, 4:8], tmp[:, 4, 0:4], MUL), sched)
                own(tt(tmp[:, 3, 0:4], tmp[:, 3, 0:4], tmp[:, 4, 4:8], ADD), sched)
                own(tt(tmp[:, 3, 0:4], tmp[:, 3, 0:4], tmp[:, 2, 4:8], ADD), sched)
                own(ts(lru_c[:, l, 0:4], tmp[:, 3, 0:4], LRU_C / 4, MUL), sched)
                r = ROWS["lru_ba"][0]
                own(ts(lru_c[:, l, 4:12], par[:, l, r:r + 8], 0.5, MUL), sched)
                r = ROWS["s5_b_glu"][0]
                own(ts(glu_hb[:, l, :], par[:, l, r:r + 4], 0.5, MUL), sched)

            with dve.Fori(0, 8) as chunk:
                for k in range(KT):
                    slot = pro_in[k % ADA_RING]
                    dve.wait_ge(slot.sem, chunk * (16 * KT // ADA_RING) + 16 * (k // ADA_RING + 1))
                    if k:
                        dve.wait_ge(pro_used.sem, pro_used.at(k, chunk))
                        op = stt(ada_acc[:, 0, :], ada_in[:, k % ADA_RING, :], cond[:, k:k + 1], ada_acc[:, 0, :],
                                 MUL, ADD)
                    else:
                        op = ts(ada_acc[:, 0, :], ada_in[:, 0, :], cond[:, 0:1], MUL)
                    op.then_inc(pro_used.sem, 1)
                dve.wait_ge(pro_sum.sem, pro_sum.at(1, chunk))
                at = bass.ds(chunk * 4, 4)
                tt(ada_t[:, 0, at], bank[0][:, 0:4], ada_b[:, 0, at], ADD).then_inc(pro_read.sem, 1)
            dve.wait_ge(pro_read.sem, 9)

            for l, s in enumerate(layers):
                pre = Signal(s.pre.sem, 0, 0)
                own(ts(hs[:, 0, :], ada_t[:, l, 16:32], 1.0, ADD), pre)
                if l == 0:
                    own(dve.tensor_copy(hs[:, 1, :], ada_t[:, l, 0:16]), pre)
                else:
                    g, b = ROWS["ln_g"][0], ROWS["ln_b"][0]
                    own(tt(hs[:, 1, :], par[:, l - 1, b:b + 16], hs[:, 0, :], MUL), pre)
                    own(tt(hs[:, 1, :], hs[:, 1, :], ada_t[:, l, 0:16], ADD), pre)
                    own(tt(hs[:, 0, :], par[:, l - 1, g:g + 16], hs[:, 0, :], MUL), pre)
                for k in range(KT):
                    dve.wait_ge(s.h_bank.sem, k + 1)
                    if k >= 2:
                        dve.wait_ge(s.op_hi.sem, k - 1)
                        dve.wait_ge(s.op_lo.sem, k - 1)
                    dve.tensor_scalar(hf[:, k % 2, :], bank[k % 4][:, :], hs[:, 0, k:k + 1], hs[:, 1, k:k + 1],
                                      MUL, ADD).then_inc(s.hf_done.sem, 1)
                dve.wait_ge(s.op_lo.sem, KT)
                dve.wait_ge(s.op_hi.sem, KT)

                branch_loop(dve, l, s, line, own, tt, ts, stt, repeat)

                post = Signal(s.post.sem, 0, 0)
                own(ts(gate1[:, :], ada_t[:, l, 32:48], 1.0, ADD), post)
                for c in range(4):
                    if c >= 2:
                        dve.wait_ge(s.gb_mm.sem, c - 1)
                    tt(diag[:, c % 2, :].rearrange("p (a b) -> p a b", a=4),
                       ident[:, :].unsqueeze(1).to_broadcast([P, 4, P]),
                       repeat(gate1[:, 4 * c:4 * c + 4], P), MUL).then_inc(s.diag.sem, 1)
                    for k in range(3 * c, 3 * c + 3):
                        dve.wait_ge(s.op_hi.sem, KT + k + 1)
                        tt(op_lo[:, k, :], y_t[:, k, :], op_hi[:, k, :].bitcast(F32), SUB).then_inc(s.op_lo.sem, 1)
                dve.wait_ge(s.glu_mm.sem, 4)
                for m in range(4):
                    dve.wait_ge(s.glu_t.sem, m + 1)
                    own(stt(glu_t[:, m, :], glu_t[:, m, :], 1.0, y_t[:, 12 + m, :], ADD, MUL), post)
                    stt(y_t[:, 12 + m, :], glu_t[:, m, :], 0.25, silu_d[:, m, :], MUL, MUL).then_inc(s.d_done.sem, 1)
                for k in range(12, 16):
                    dve.wait_ge(s.op_hi.sem, KT + k + 1)
                    tt(op_lo[:, k, :], y_t[:, k, :], op_hi[:, k, :].bitcast(F32), SUB).then_inc(s.op_lo.sem, 1)

                dve.wait_ge(s.gb.sem, 4)
                dve.wait_ge(s.z_in.sem, 16 * (1 + (2 if l else 0) + (2 if l == DEPTH - 1 else 0)))
                for c in range(4):
                    w = slice(S * c, S * (c + 1))
                    for t in range(ST):
                        if l:
                            own(tt(z[:, t, w], z[:, t, w], ln_prev[:, 0, w], MUL), post)
                            own(tt(z[:, t, w], z[:, t, w], ln_prev[:, 1, w], ADD), post)
                        if t < ST - 1:
                            dve.wait_ge(s.y_mm.sem, 3 * c + t + 1)
                        else:
                            dve.wait_ge(s.mm_done.sem, s.mm_done.at(8 * (c + 1), CT))
                        tt(mix, bank[4 * (c % 2) + t][:, :], gate_b[:, c, :], MUL).then_inc(s.y_used.sem, 1)
                        dve.wait_ge(s.y_used.sem, 4 * c + t + 1)
                        own(stt(z[:, t, w], z[:, t, w], ALPHA, mix, MUL, ADD), post)
                        own(dve.bn_stats(stats[:, t, c, :], z[:, t, w]), post)
                        if c == 3:
                            line(dve.bn_aggr(mv[:, t, 0:2], stats[:, t, :, :]), s.var)
                for t in range(ST):
                    dve.wait_ge(s.std.sem, t + 1)
                    own(dve.reciprocal(mv[:, t, 3:4], mv[:, t, 2:3]), post)
                    norm = dve.tensor_scalar(z[:, t, :], z[:, t, :], mv[:, t, 0:1], mv[:, t, 3:4], SUB, MUL)
                    if l == DEPTH - 1:
                        own(norm, post)
                        own(tt(z[:, t, :], z[:, t, :], ln_last[:, 0, :], MUL), post)
                        norm = tt(z[:, t, :], z[:, t, :], ln_last[:, 1, :], ADD)
                    norm.then_inc(s.xn.sem, 1)
                dve.wait_ge(s.xn.sem, ST)


_INS = ("x", "c", "rel_bias", "w_ada", "b_ada", "w_in", "conv_a", "conv_c", "conv_c_b", "lru_wa", "lru_ba",
        "lru_wx", "lru_bx", "lru_lambda", "s5_lam_re", "s5_lam_im", "s5_log_dt", "s5_b_re", "s5_b_im",
        "s5_c_re", "s5_c_im", "s5_d", "s5_w_glu", "s5_b_glu", "w_out", "ln_g", "ln_b")


def kernel(**inputs):
    import concourse.bacc as bacc
    from concourse.bass_utils import run_bass_kernel_spmd

    nc = bacc.Bacc("TRN2", target_bir_lowering=False, num_devices=1)
    arrays, drams = {}, {}
    for name in _INS:
        a = np.ascontiguousarray(inputs[name])
        arrays["in_" + name] = a
        drams[name] = nc.dram_tensor("in_" + name, a.shape, mybir.dt.from_np(a.dtype), kind="ExternalInput").ap()
    out = nc.dram_tensor("out", (1, S, D), F32, kind="ExternalOutput").ap()
    trunk(nc, drams, out)
    return run_bass_kernel_spmd(nc, [arrays], core_ids=[0]).results[0]["out"]
```

```python
import math
from contextlib import ExitStack

import numpy as np
import concourse.bass as bass
from concourse import mybir

F32 = mybir.dt.float32
F32R = mybir.dt.float32r
I32 = mybir.dt.int32
ALU = mybir.AluOpType
ACT = mybir.ActivationFunctionType
AX_X = mybir.AxisListType.X

P = 128
D = 2048
S = 512
DEPTH = 2
BR = D // 4
KT = D // P
CT = BR // P
ST = S // P
N_IN = 12 * BR
HEADS = 8
HD = BR // HEADS
CH = 16
NS = 64
SQ = 4
TC = P
ALPHA = (2 * DEPTH) ** 0.25
EPS = 1e-5
NEG = -1e30
ROUND = 12582912.0
TWO_PI = 6.2831845
LRU_C = 8.0
GELU_C = math.sqrt(2 / math.pi)

UNITS = ("d_u", "c_x", "q", "k", "v", "c_g", "d_g", "a_c", "a_x", "b_g", "a_g", "a_b")
COLUMN = dict(a_b=0, a_c=1, a_x=2, a_g=3, q=4, k=5, v=6, b_g=7, c_x=8, c_g=9, d_u=10, d_g=11)
HALF = 2 * len(UNITS)
KH = KT // 2
NRAW, NHL = 3, 2
FIRST_SPLIT = (12, 12)
W_OUT = 32
ADA_RING = 4
PRO_RING = 8
ADA_CHUNKS = (((0, 32), (1, 0), (1, 16)), ((1, 32),))
ADA_LOADS = ({4: 4, 6: 4, 7: 4, 10: 4, 14: 3, 16: 1, 18: 4, 21: 5, 22: 4, 23: 15},
             {4: 4, 7: 1, 8: 1, 11: 2, 14: 1, 17: 1, 18: 1, 21: 1, 22: 2, 23: 2})
OWN_STEPS = (169, 167)

ROWS = {}
_n = 0
for _name, _rows in (("conv_a", 12), ("conv_c", 16), ("conv_c_b", 4), ("lru_ba", 4), ("lru_bx", 4),
                     ("lru_lambda", 4), ("s5_d", 4), ("s5_b_glu", 4), ("ln_g", 16), ("ln_b", 16),
                     ("s5_lam_re", 16), ("s5_lam_im", 16)):
    ROWS[_name] = (_n, _rows)
    _n += _rows
N_ROWS = _n


def bucket_of(d):
    if d < 16:
        return d
    return min(31, 16 + int(np.float32(math.log(d / 16) / math.log(128)) * np.float32(16)))


class Signal:

    def __init__(self, sem, per=0, first=0):
        self.sem, self.per, self.first, self.local = sem, per, first, 0

    def at(self, n, step=0):
        return step * self.per + (self.first + n)


class Line:

    def __init__(self, eng):
        self.eng, self.step, self.last = eng, 0, None

    def __call__(self, ins, sig, n=1):
        ins.then_inc(sig.sem, n)
        sig.local += n
        self.last = sig
        return ins

    def settle(self):
        self.eng.wait_ge(self.last.sem, self.last.at(self.last.local, self.step))

    def enter(self, step, *sigs):
        self.step = step
        for s in sigs:
            s.local = 0


def trunk(nc, A, out):
    x_norm = nc.dram_tensor("x_norm_scratch", (S, D), F32, kind="Internal").ap()
    bias_row_d = nc.dram_tensor("bias_row_scratch", (HEADS, 640), F32, kind="Internal").ap()
    bias_d = nc.dram_tensor("bias_tile_scratch", (HEADS, P, S), F32, kind="Internal").ap()

    with ExitStack() as ctx:
        def sb(name, shape, dt=F32):
            return ctx.enter_context(nc.sbuf_tensor(name, shape, dt))

        def signal(name, per=0, first=0):
            return Signal(ctx.enter_context(nc.semaphore(name)), per, first)

        op_hi = sb("op_hi", [P, KT, S], F32R)
        op_lo = sb("op_lo", [P, KT, S], F32R)
        y_t = sb("y_t", [P, KT, S])
        z = y_t[:, :, :].rearrange("p (s n) t -> p s (n t)", s=ST)
        raw = sb("raw", [P, NRAW, KH * P])
        w_hi = sb("w_hi", [P, NHL, KH * P], F32R)
        w_lo = sb("w_lo", [P, NHL, KH * P], F32R)
        ada_in = sb("ada_in", [P, ADA_RING, S])
        ada_acc = sb("ada_acc", [P, 3, S])
        work = sb("work", [P, 24, S])
        bias_t = sb("bias_t", [P, 2, S])
        rot = sb("rot", [P, 2, SQ, TC])
        s5_w = sb("s5_w", [P, 4, P])
        s5_bb = sb("s5_bb", [P, 2, SQ, 2, CH])
        s5_k = sb("s5_k", [P, 4, SQ])
        lru_w = sb("lru_w", [P, 2, P])
        xp = sb("xp", [P, 3 + S])
        va = sb("va", [P, 2 + S])
        ident = sb("ident", [P, P])
        ones = sb("ones", [P, P])
        j_row = sb("j_row", [P, TC])
        par = sb("par", [P, DEPTH, N_ROWS])
        ada_b = sb("ada_b", [P, DEPTH, 64])
        dt_in = sb("dt_in", [16, DEPTH, 2])
        dt_t = sb("dt_t", [P, DEPTH, 16])
        mask = sb("mask", [P, 4])
        ada_t = sb("ada_t", [P, DEPTH, 48])
        cond = sb("cond", [P, 16])
        s5c = sb("s5c", [P, DEPTH, 4, 16])
        lru_c = sb("lru_c", [P, DEPTH, 12])
        glu_hb = sb("glu_hb", [P, DEPTH, 4])
        hs = sb("hs", [P, 2, KT])
        gate1 = sb("gate1", [P, KT])
        rel = sb("rel", [HEADS, 32])
        soft = sb("soft", [P, 4, 4])
        carry = sb("carry", [P, 4])
        spare = sb("spare", [P, 1])
        stats = sb("stats", [P, ST, 4, 6])
        mv = sb("mv", [P, ST, 4])
        consts = sb("consts", [P, 2])

        u_d, xc, q_t, k_t, v_t = (work[:, i, :] for i in range(5))
        s5_s = [work[:, 5 + i, :] for i in range(5)]
        s5_cc = s5_s[3][:, 0:256].rearrange("p (i g s) -> p i g s", i=2, g=2)
        s5_raw = s5_s[4][:, 0:256].rearrange("p (i s) -> p i s", i=4)
        w_glu = work[:, 5:9, :]
        v_s = work[:, 10, :].rearrange("p (k d) -> p k d", k=ST)
        prob = work[:, 11:14, :].rearrange("p a b -> p (a b)")
        lru_s = [work[:, 11 + i, :] for i in range(3)]
        p_t = work[:, 14:16, :]
        gx = work[:, 16:18, :]
        gt = work[:, 18:20, :]
        silu_d = work[:, 20:24, :]
        ax = xp[:, 3:3 + S]
        gel = v_t
        gate_b = work[:, 0:4, :]
        glu_t = work[:, 14:18, :]
        ln_prev = work[:, 4:12, :].rearrange("p (i a) b -> p i (a b)", i=2)
        ln_last = work[:, 14:22, :].rearrange("p (i a) b -> p i (a b)", i=2)
        mix = work[:, 13, :]
        hf = work[:, 16:18, :]
        diag = work[:, 18:20, :]
        brow = work[0:HEADS, 8:11, :].rearrange("p a b -> p (a b)")[:, 0:1280].rearrange("p (a b) -> p a b", a=2)
        rows = [work[:, 20 + 2 * l, P * l:P * l + 2 * P].rearrange("p (a b) -> p a b", a=2) for l in range(DEPTH)]
        flip, mask_row = work[:, 21, 0:P], work[0:32, 21, P:2 * P]
        dt_row = [work[0:16, 21, P * (2 + l):P * (3 + l)] for l in range(DEPTH)]
        j_int = work[:, 22, 0:TC].bitcast(I32)
        tmp = work[:, 23, 0:P].rearrange("p (a b) -> p a b", a=8)
        pro_ring = [raw[:, i, :].rearrange("p (i n) -> p i n", i=2) for i in range(NRAW)]
        pro_ring += [ada_in[:, 0:2, :], ada_in[:, 2:4, :], bias_t[:, :, :], diag,
                     rot[:, :, :, :].rearrange("p i q t -> p i (q t)")]
        P_AT = [0, 128, 384, 768]
        bank = [ctx.enter_context(nc.psum_tensor(f"bank{i}", [P, S], F32)) for i in range(8)]

        const_done = signal("const_done")
        setup_dma = signal("setup_dma")
        row_dma = [signal(f"row_dma{l}") for l in range(DEPTH)]
        turned = signal("turned")
        setup_own = signal("setup_own")
        bias_own = signal("bias_own")
        param_own = signal("param_own")
        setup_dve = signal("setup_dve")
        setup_act = signal("setup_act")
        bias_row = signal("bias_row")
        bias_io = signal("bias_io")
        bias_mm = signal("bias_mm")
        bias_done = signal("bias_done")
        x_io = signal("x_io")
        out_dma = signal("out_dma")
        pro_in = [signal(f"pro_in{i}") for i in range(PRO_RING)]
        pro_used = signal("pro_used")
        pro_sum = signal("pro_sum")

        class Layer:
            pass
        layers = []
        for l in range(DEPTH):
            s, n = Layer(), f"_{l}"
            s.raw_in = [signal(f"raw_in{i}" + n, HALF // NRAW * 16) for i in range(NRAW)]
            s.hi_done = signal("hi_done" + n, HALF)
            s.lo_done = signal("lo_done" + n, HALF, NRAW)
            s.mm_done = signal("mm_done" + n, HALF, NHL)
            full = [0, 0, SQ, SQ, 1, 10, 9, 1]
            free = [6, 6, SQ, SQ, 2, 6, 5, 2]
            s.full = [signal(f"full{b}" + n, full[b]) if full[b] else None for b in range(8)]
            s.free = [signal(f"free{b}" + n, free[b], 1) for b in range(8)]
            s.step_in = signal("step_in" + n, 160)
            s.pre, s.post = signal("dve_pre" + n), signal("dve_post" + n)
            s.own = signal("dve_own" + n, OWN_STEPS[l])
            s.act_own = signal("act_own" + n, 1)
            s.to_act = signal("to_act" + n, 4)
            s.from_act = signal("from_act" + n, 5)
            s.bb_done = signal("bb_done" + n, 1)
            s.xc_done = signal("xc_done" + n, 1)
            s.x_rot = signal("x_rot" + n, SQ)
            s.c_done = signal("c_done" + n, SQ, 1)
            s.p_norm = signal("p_norm" + n, 2)
            s.p_copy = signal("p_copy" + n, 8, 1)
            s.pv_done = signal("pv_done" + n, 8, 1)
            s.gate_used = [signal(f"gate_used{i}" + n, 2, 1) for i in range(2)]
            s.step_end = signal("step_end" + n, 1, 1)
            s.ada = KT * len(ADA_CHUNKS[l])
            s.ada_in = [signal(f"ada_in{i}" + n, s.ada // ADA_RING * 16) for i in range(ADA_RING)]
            s.ada_used = signal("ada_used" + n, s.ada, ADA_RING)
            s.from_one = [s.c_done, s.p_copy, s.pv_done, s.step_end, *s.gate_used, *s.free]
            s.h_bank = signal("h_bank" + n)
            s.hf_done = signal("hf_done" + n)
            s.op_hi = signal("op_hi_done" + n)
            s.op_lo = signal("op_lo_done" + n)
            s.glu_in = signal("glu_in" + n)
            s.glu_mm = signal("glu_mm" + n)
            s.glu_t = signal("glu_t" + n)
            s.diag = signal("diag" + n)
            s.gb_mm = signal("gb_mm" + n)
            s.gb = signal("gb" + n)
            s.z_in = signal("z_in" + n)
            s.ln_in = signal("ln_in" + n)
            s.y_mm = signal("y_mm" + n)
            s.y_used = signal("y_used" + n)
            s.d_done = signal("d_done" + n)
            s.var = signal("var" + n)
            s.std = signal("std" + n)
            s.xn = signal("xn" + n)
            layers.append(s)

        w_in_v = A["w_in"].rearrange("l (k p) n -> l p k n", p=P)
        w_out_v = A["w_out"].rearrange("l (k p) n -> l p k n", p=P)
        w_ada_v = A["w_ada"].rearrange("l (k p) n -> l k p n", p=P)
        x_v = A["x"].rearrange("b (s p) n -> p (b s) n", p=P)
        xn_v = x_norm.rearrange("(s p) n -> p s n", p=P)
        out_v = out.rearrange("b (s p) n -> p (b s) n", p=P)

        def unit_copied(eng, s, name, ct):
            u = UNITS.index(name)
            eng.wait_ge(s.free[u % 2].sem, s.free[u % 2].at(u // 2 + 1, ct))

        block = ctx.enter_context(nc.Block())

        @block.sync
        def _(sp):
            sp.dma_start(rel[:, :], A["rel_bias"].rearrange("b h -> h b"),
                         allow_slow_non_contiguous=True).then_inc(setup_dma.sem, 16)
            def parameters(l):
                for name, (at, n) in ROWS.items():
                    if name in ("s5_lam_re", "s5_lam_im"):
                        src = A[name][l].rearrange("(s g) p -> s (g p)", g=2)
                    elif name in ("conv_a", "conv_c"):
                        src = A[name][l].rearrange("k (t p) -> (k t) p", p=P)
                    else:
                        src = A[name][l].rearrange("(t p) -> t p", p=P)
                    sp.dma_start(rows[l][at:at + n, 0, :], src).then_inc(row_dma[l].sem, 16)
                sp.dma_start(rows[l][0:48, 1, :], A["b_ada"][l].rearrange("(t p) -> t p", p=P)).then_inc(row_dma[l].sem, 16)
                sp.dma_start(rows[l][48:64, 1, :], A["c"].rearrange("b (t p) -> (b t) p", p=P)).then_inc(row_dma[l].sem, 16)
                sp.dma_start(dt_in[:, l, :], A["s5_log_dt"][l].rearrange("(s g) -> s g", g=2)).then_inc(row_dma[l].sem, 16)
            parameters(0)
            for a in range(4 * KT):
                chunk, k = a // KT, a % KT
                if a == PRO_RING:
                    parameters(1)
                    sp.wait_ge(bias_row.sem, 1)
                    sp.dma_start(bias_row_d, brow[:, 0, :]).then_inc(bias_io.sem, 16)
                if a == PRO_RING + 2:
                    sp.wait_ge(bias_io.sem, 16)
                    for h in range(HEADS):
                        src = bass.AP(tensor=bias_row_d.tensor, offset=bias_row_d[h, 0:1].offset, ap=[[1, P], [1, S]])
                        sp.dma_start(work[:, h, :], src).then_inc(bias_io.sem, 16)
                if a == PRO_RING + 4:
                    sp.dma_start(z, x_v).then_inc(x_io.sem, 16)
                if a >= PRO_RING:
                    sp.wait_ge(pro_used.sem, a - PRO_RING + 1)
                sp.dma_start(pro_ring[a % PRO_RING],
                             w_ada_v[0, k, :, 0:4 * BR * 2].rearrange("p (i n) -> p i n", i=2)
                             [:, :, chunk * S:(chunk + 1) * S]).then_inc(pro_in[a % PRO_RING].sem, 16)
            sp.wait_ge(bias_done.sem, HEADS)
            sp.dma_start(bias_d.rearrange("h p t -> p h t"), work[:, 8:16, :]).then_inc(bias_io.sem, 16)

            for l, s in enumerate(layers):
                if l == 0:
                    sp.wait_ge(pro_used.sem, 4 * KT - PRO_RING + NRAW)
                else:
                    sp.wait_ge(layers[l - 1].lo_done.sem, layers[l - 1].lo_done.at(W_OUT, CT))
                with sp.Fori(0, CT) as ct:
                    for n in range(HALF):
                        at = ct * P + COLUMN[UNITS[n // 2]] * BR
                        if n != HALF - 2:
                            sp.wait_ge(s.lo_done.sem, ct * HALF + (n + 1 + (n == HALF - 3)))
                        sp.dma_start(raw[:, n % NRAW, :].rearrange("p (k n) -> p k n", k=KH),
                                     w_in_v[l, :, (n % 2) * KH:(n % 2 + 1) * KH,
                                            bass.ds(at, P)])\
                            .then_inc(s.raw_in[n % NRAW].sem, 16)
                        if n == 4:
                            if l == 0:
                                sp.wait_ge(bias_io.sem, 16 * 10)
                                sp.wait_ge(pro_used.sem, 4 * KT)
                            sp.wait_ge(s.step_end.sem, s.step_end.at(0, ct))
                            for i, name in enumerate(("s5_b_re", "s5_b_im")):
                                src = A[name][l].rearrange("(s g) p c -> (g p) s c", g=2)
                                sp.dma_start(s5_raw[:, i, :].rearrange("p (s c) -> p s c", s=SQ),
                                             src[:, bass.ds(ct * SQ, SQ), :]).then_inc(s.step_in.sem, 16)
                            for i, name in enumerate(("s5_c_re", "s5_c_im")):
                                src = A[name][l].rearrange("g c p -> (g c) p")
                                sp.dma_start(s5_raw[:, 2 + i, :], src[bass.ds(ct * P, P), :])\
                                    .then_inc(s.step_in.sem, 16)
                            for i, name in enumerate(("lru_wa", "lru_wx")):
                                src = A[name][l].rearrange("h i j -> (h i) j")
                                for h in range(2):
                                    sp.dma_start(lru_w[64 * h:64 * h + 64, i, 64 * h:64 * h + 64],
                                                 src[bass.ds(ct * P + 64 * h, 64), :]).then_inc(s.step_in.sem, 16)
                            for h in range(2):
                                sp.dma_start(bias_t[:, h, :],
                                             bias_d[bass.ds(ct * 2 + h, 1)].rearrange("o p t -> (o p) t"))\
                                    .then_inc(s.step_in.sem, 16)
                        before = sum(count for at_, count in ADA_LOADS[l].items() if at_ < n)
                        for a in range(before, before + ADA_LOADS[l].get(n, 0)):
                            chunk, k = a // KT, a % KT
                            sp.wait_ge(s.ada_used.sem, ct * s.ada + (a + 1))
                            of, part = ADA_CHUNKS[l][chunk]
                            sp.dma_start(ada_in[:, a % ADA_RING, :],
                                         w_ada_v[of, k, :, bass.ds(ct * S + part * P, S)])\
                                .then_inc(s.ada_in[a % ADA_RING].sem, 16)
                for n in range(W_OUT):
                    chunk, kk = n // 8, n % 8
                    sp.wait_ge(s.lo_done.sem, s.lo_done.at(n + 1 - NRAW, CT))
                    sp.dma_start(raw[:, n % NRAW, :].rearrange("p (k n) -> p k n", k=2),
                                 w_out_v[l, :, 2 * kk:2 * kk + 2, chunk * S:(chunk + 1) * S])\
                        .then_inc(s.raw_in[n % NRAW].sem, 16)
                    if n == NRAW - 1:
                        sp.wait_ge(s.step_end.sem, s.step_end.at(0, CT))
                        sp.dma_start(w_glu, A["s5_w_glu"][l].rearrange("(k p) n -> p k n", p=P))\
                            .then_inc(s.glu_in.sem, 16)
                    if 6 <= n < 6 + ST:
                        if n == 6:
                            sp.wait_ge(s.op_hi.sem, 2 * KT)
                            sp.wait_ge(s.op_lo.sem, 2 * KT)
                            if l:
                                sp.wait_ge(x_io.sem, 16 * (1 + ST))
                        sp.dma_start(z[:, n - 6, :], (xn_v if l else x_v)[:, n - 6, :]).then_inc(s.z_in.sem, 16)
                    for i, name in ((0, "ln_g"), (1, "ln_b")):
                        if l and n == 6 + ST + i:
                            sp.dma_start(ln_prev[:, i, :], A[name][l - 1].partition_broadcast(P))\
                                .then_inc(s.z_in.sem, 16)
                        if l == DEPTH - 1 and n == 8 + ST + i:
                            sp.dma_start(ln_last[:, i, :], A[name][l].partition_broadcast(P))\
                                .then_inc(s.ln_in.sem, 16)
                if l < DEPTH - 1:
                    for t in range(ST):
                        sp.wait_ge(s.xn.sem, t + 1)
                        sp.dma_start(xn_v[:, t, :], z[:, t, :]).then_inc(x_io.sem, 16)
                else:
                    for t in range(ST):
                        sp.wait_ge(s.xn.sem, t + 1)
                        sp.dma_start(out_v[:, t, :], z[:, t, :]).then_inc(out_dma.sem, 16)
                    sp.wait_ge(out_dma.sem, 16 * ST)

        @block.gpsimd
        def _(pool):
            for sig in (*layers[0].from_one, *layers[1].from_one):
                pool.sem_inc(sig.sem, 1)
            pool.memset(ident[:, :], 0.0).then_inc(const_done.sem, 1)
            pool.memset(flip[:, :], 0.0).then_inc(const_done.sem, 1)
            pool.memset(mask_row[:, :], 0.0).then_inc(const_done.sem, 1)
            pool.wait_ge(const_done.sem, 3)
            pool.affine_select(out=ident[:, :], in_=ident[:, :], compare_op=ALU.not_equal, fill=1.0, base=0,
                               pattern=[[-1, P]], channel_multiplier=1).then_inc(const_done.sem, 1)
            pool.affine_select(out=flip[:, :], in_=flip[:, :], compare_op=ALU.not_equal, fill=1.0, base=-(P - 1),
                               pattern=[[1, P]], channel_multiplier=1).then_inc(const_done.sem, 1)
            pool.memset(mask_row[:, :].rearrange("p (a b c) -> p a b c", b=2, c=CH)[:, :, 0, :], 1.0)\
                .then_inc(const_done.sem, 1)
            pool.iota(j_int[:, :], pattern=[[1, TC]], base=1, channel_multiplier=0).then_inc(const_done.sem, 1)
            pool.memset(ones[:, :], 1.0).then_inc(const_done.sem, 1)
            pool.memset(lru_w[:, :, :], 0.0).then_inc(const_done.sem, 1)
            pool.memset(xp[:, 0:3], 0.0).then_inc(const_done.sem, 1)
            pool.memset(va[:, 0:2], 0.0).then_inc(const_done.sem, 1)
            pool.memset(s5_bb[:, :, :, :, :], 0.0).then_inc(const_done.sem, 1)
            pool.memset(consts[:, 0:1], math.pi / 2).then_inc(const_done.sem, 1)
            pool.memset(consts[:, 1:2], EPS).then_inc(const_done.sem, 1)

            rows_line = Line(pool)
            row_done = Signal(bias_own.sem, 0, 0)

            def row_op(ins):
                rows_line(ins, row_done)
                rows_line.settle()

            pool.wait_ge(setup_dma.sem, 16)
            last = S - 1
            near = last - P
            row_op(pool.memset(brow[:, :, :], NEG))
            row_op(pool.memset(brow[:, 1, 3:S:4], 0.0))
            row_op(pool.memset(brow[:, 1, 15:S:16], math.log(2)))
            row_op(pool.memset(brow[:, 1, near:S], 0.0))
            row_op(pool.memset(brow[:, 1, near:S:4], math.log(2)))
            row_op(pool.memset(brow[:, 1, near:S:16], math.log(3)))
            d = 0
            while d < S:
                e = d
                while e + 1 < S and bucket_of(e + 1) == bucket_of(d):
                    e += 1
                k = bucket_of(d)
                row_op(pool.tensor_copy(brow[:, 0, last - e:last - d + 1],
                                       rel[:, k:k + 1].to_broadcast([HEADS, e - d + 1])))
                d = e + 1
            pool.tensor_tensor(brow[:, 0, 0:S], brow[:, 0, 0:S], brow[:, 1, 0:S], ALU.add).then_inc(bias_row.sem, 1)


            for l, s in enumerate(layers):
                pool.sem_inc(s.lo_done.sem, NRAW)
                def split_lo(n, step, ahead=0):
                    pool.wait_ge(s.hi_done.sem, s.hi_done.at(n + 1, step) + ahead * HALF)
                    pool.wait_ge(s.mm_done.sem, s.mm_done.at(n + 1 - NHL, step) + ahead * HALF)
                    pool.tensor_tensor(w_lo[:, n % NHL, :], raw[:, n % NRAW, :],
                                       w_hi[:, n % NHL, :].bitcast(F32), ALU.subtract).then_inc(s.lo_done.sem, 1)

                for k in range(KT):
                    if k == FIRST_SPLIT[l]:
                        split_lo(0, 0)
                        split_lo(1, 0)
                    pool.wait_ge(s.op_hi.sem, k + 1)
                    pool.tensor_tensor(op_lo[:, k, :], hf[:, k % 2, :], op_hi[:, k, :].bitcast(F32),
                                       ALU.subtract).then_inc(s.op_lo.sem, 1)

                with pool.Fori(0, CT) as ct:
                    for n in range(2, HALF):
                        split_lo(n, ct)
                    split_lo(0, ct, 1)
                    split_lo(1, ct, 1)
                for n in range(2, W_OUT):
                    split_lo(n, CT)

        @block.scalar
        def _(act):
            act.wait_ge(setup_dve.sem, 1)
            act.activation(cond[:, :], ada_b[:, 0, 48:64], ACT.Tanh, scale=0.5).then_inc(setup_act.sem, 1)

            def parameters(l):
                act.wait_ge(setup_dve.sem, 3 * l + 2)
                act.activation(dt_t[:, l, :], dt_t[:, l, :], ACT.Exp).then_inc(setup_act.sem, 1)
                act.wait_ge(setup_dve.sem, 3 * l + 3)
                act.activation(tmp[:, 2, 0:4], tmp[:, 2, 0:4], ACT.Exp).then_inc(setup_act.sem, 1)
                act.activation(tmp[:, 0, :], tmp[:, 0, :], ACT.Tanh, scale=0.5).then_inc(setup_act.sem, 1)
                act.activation(tmp[:, 5, :], tmp[:, 1, :], ACT.Sin, scale=TWO_PI).then_inc(setup_act.sem, 1)
                act.activation(tmp[:, 6, :], tmp[:, 1, :], ACT.Sin, scale=TWO_PI / 2).then_inc(setup_act.sem, 1)
                act.wait_ge(setup_dve.sem, 3 * l + 4)
                act.activation(tmp[:, 3, 0:4], tmp[:, 3, 0:4], ACT.Ln).then_inc(setup_act.sem, 1)
                act.wait_ge(setup_act.sem, 7 * l + 7)
                act.activation(tmp[:, 4, 0:4], tmp[:, 3, 0:4], ACT.Tanh, scale=0.5).then_inc(setup_act.sem, 1)

            parameters(0)
            for h in range(HEADS):
                act.wait_ge(bias_mm.sem, h + 1)
                act.activation(work[:, 8 + h, :], bank[3 + h % 4][:, :], ACT.Copy).then_inc(bias_done.sem, 1)
            parameters(1)

            for l, s in enumerate(layers):
                def split_hi(n, step, ahead=0):
                    slot = s.raw_in[n % NRAW]
                    act.wait_ge(slot.sem, slot.at(16 * (n // NRAW + 1), step) + ahead * slot.per)
                    act.wait_ge(s.mm_done.sem, s.mm_done.at(n + 1 - NHL, step) + ahead * HALF)
                    act.activation(w_hi[:, n % NHL, :], raw[:, n % NRAW, :], ACT.Copy).then_inc(s.hi_done.sem, 1)

                for k in range(KT):
                    if k == FIRST_SPLIT[l]:
                        split_hi(0, 0)
                        split_hi(1, 0)
                    act.wait_ge(s.hf_done.sem, k + 1)
                    act.activation(op_hi[:, k, :], hf[:, k % 2, :], ACT.Copy).then_inc(s.op_hi.sem, 1)

                with act.Fori(0, CT) as ct:
                    def unit(name):
                        u = UNITS.index(name)
                        act.wait_ge(s.mm_done.sem, s.mm_done.at(2 * u + 2, ct))
                        return bank[u % 2][:, :], s.free[u % 2]

                    def copy(name, dst, scale=1.0):
                        ps, free = unit(name)
                        act.activation(dst, ps, ACT.Copy, scale=scale).then_inc(free.sem, 1)

                    def gate(name, i, use):
                        ps, free = unit(name)
                        act.wait_ge(s.gate_used[i].sem, s.gate_used[i].at(use, ct))
                        act.activation(gt[:, i, :], ps, ACT.Tanh, scale=0.5)
                        act.activation(gx[:, i, :], ps, ACT.Copy).then_inc(free.sem, 1)

                    def exps(h):
                        act.wait_ge(s.to_act.sem, s.to_act.at(2 + h, ct))
                        for t in range(ST):
                            pr = prob[:, P_AT[t]:P_AT[t] + P * (t + 1)]
                            e = act.activation(pr, pr, ACT.Exp, bias=soft[:, 1, t:t + 1], scale=1.0,
                                               accum_out=soft[:, 2, t:t + 1])
                        e.then_inc(s.from_act.sem, 1)

                    def p_copy(h, kb):
                        b, i = 5 + kb % 2, 4 * h + kb
                        use = 1 + 4 * h + 2 + kb // 2
                        act.wait_ge(s.full[b].sem, s.full[b].at(use + 1, ct))
                        act.wait_ge(s.pv_done.sem, s.pv_done.at(max(0, i - 1), ct))
                        act.activation(p_t[:, kb % 2, 0:P * (ST - kb)], bank[b][:, 0:P * (ST - kb)], ACT.Copy)\
                            .then_inc(s.p_copy.sem, 1)

                    def lru():
                        act.wait_ge(s.full[5].sem, s.full[5].at(1, ct))
                        act.wait_ge(s.full[6].sem, s.full[6].at(1, ct))
                        act.activation(lru_s[0], bank[5][:, :], ACT.Tanh, scale=0.5,
                                       bias=lru_c[:, l, bass.ds(ct + 4, 1)]).then_inc(s.free[5].sem, 1)
                        act.activation(lru_s[1], bank[6][:, :], ACT.Tanh, scale=0.5,
                                       bias=lru_c[:, l, bass.ds(ct + 8, 1)]).then_inc(s.free[6].sem, 1)
                        act.wait_ge(s.free[5].sem, s.free[5].at(1, ct))
                        act.activation(lru_s[0], lru_s[0], ACT.Tanh, scale=lru_c[:, l, bass.ds(ct, 1)],
                                       bias=lru_c[:, l, bass.ds(ct, 1)]).then_inc(s.act_own.sem, 1)
                        act.wait_ge(s.act_own.sem, s.act_own.at(1, ct))
                        act.activation(lru_s[2], lru_s[0], ACT.Sqrt).then_inc(s.from_act.sem, 1)

                    def rotation():
                        act.wait_ge(s.to_act.sem, s.to_act.at(1, ct))
                        act.activation(rot[:, 0, :, :], rot[:, 0, :, :], ACT.Sin, scale=TWO_PI)
                        act.activation(rot[:, 1, :, :], rot[:, 1, :, :], ACT.Sin, scale=-TWO_PI,
                                       bias=consts[:, 0:1]).then_inc(s.from_act.sem, 1)
                        act.wait_ge(s.full[4].sem, s.full[4].at(1, ct))
                        act.activation(s5_w[:, :, :].rearrange("p a b -> p (a b)"), bank[4][:, :], ACT.Copy)\
                            .then_inc(s.free[4].sem, 1)

                    for n in range(2, HALF):
                        split_hi(n, ct)
                        if n == 3:
                            act.wait_ge(s.free[4].sem, s.free[4].at(0, ct))
                            copy("d_u", u_d)
                        if n == 5:
                            act.wait_ge(s.step_end.sem, s.step_end.at(0, ct))
                            copy("c_x", xp[:, 3:3 + S])
                            rotation()
                        if n == 7:
                            copy("q", q_t, HD ** -0.5)
                        if n == 8:
                            lru()
                        if n == 9:
                            copy("k", k_t)
                        if n == 11:
                            copy("v", v_t)
                        if n == 13:
                            exps(0)
                            gate("c_g", 0, 0)
                        if n == 14:
                            act.wait_ge(s.full[7].sem, s.full[7].at(s.full[7].per, ct))
                            act.wait_ge(s.pv_done.sem, s.pv_done.at(0, ct))
                            act.activation(work[:, 10, :], bank[7][:, :], ACT.Copy).then_inc(s.free[7].sem, 1)
                        if n == 15:
                            gate("d_g", 1, 0)
                        if n == 16:
                            p_copy(0, 0)
                            p_copy(0, 1)
                        if n == 17:
                            p_copy(0, 2)
                            p_copy(0, 3)
                            copy("a_c", va[:, 2:2 + S])
                        if n == 19:
                            copy("a_x", ax)
                        if n == 20:
                            exps(1)
                        if n == 21:
                            gate("b_g", 0, 1)
                        if n == 23:
                            p_copy(1, 0)
                            p_copy(1, 1)
                            gate("a_g", 1, 1)

                    p_copy(1, 2)
                    p_copy(1, 3)
                    split_hi(0, ct, 1)
                    split_hi(1, ct, 1)
                    act.wait_ge(s.to_act.sem, s.to_act.at(4, ct))
                    act.activation(gel, gel, ACT.Tanh, scale=GELU_C).then_inc(s.from_act.sem, 1)

                act.wait_ge(s.mm_done.sem, s.mm_done.at(0, CT))
                act.wait_ge(s.step_end.sem, s.step_end.at(0, CT))
                for k in range(12):
                    act.activation(op_hi[:, k, :], y_t[:, k, :], ACT.Copy).then_inc(s.op_hi.sem, 1)
                for m in range(4):
                    act.wait_ge(s.glu_mm.sem, m + 1)
                    act.activation(glu_t[:, m, :], bank[4 + m][:, :], ACT.Tanh, scale=0.5,
                                   bias=glu_hb[:, l, m:m + 1]).then_inc(s.glu_t.sem, 1)
                for c in range(4):
                    act.wait_ge(s.gb_mm.sem, c + 1)
                    act.activation(gate_b[:, c, :], bank[4 + c][:, :], ACT.Copy).then_inc(s.gb.sem, 1)
                for m in range(4):
                    act.wait_ge(s.d_done.sem, m + 1)
                    act.activation(op_hi[:, 12 + m, :], y_t[:, 12 + m, :], ACT.Copy).then_inc(s.op_hi.sem, 1)
                for n in range(2, W_OUT):
                    split_hi(n, CT)
                for t in range(ST):
                    act.wait_ge(s.var.sem, t + 1)
                    act.activation(mv[:, t, 2:3], mv[:, t, 1:2], ACT.Sqrt, bias=consts[:, 1:2], scale=1.0)\
                        .then_inc(s.std.sem, 1)

        @block.tensor
        def _(pe):
            def turn(out_, in_, sig):
                n = in_.shape[0]
                return pe.transpose(out_, in_, ident[0:n, 0:n]).then_inc(sig.sem, 1)

            pe.wait_ge(const_done.sem, 14)
            for l in range(DEPTH):
                pe.wait_ge(row_dma[l].sem, 16 * 15)
                if l:
                    pe.wait_ge(setup_dve.sem, 2)
                turn(bank[0][:, 0:N_ROWS], rows[l][0:N_ROWS, 0, :], turned)
                turn(bank[1][:, 0:64], rows[l][0:64, 1, :], turned)
                pe.wait_ge(setup_own.sem, l + 1)
                turn(bank[2][:, 0:16], dt_row[l][:, :], turned)
                if l == 0:
                    turn(bank[3][:, 0:32], mask_row[:, :], turned)
            pe.wait_ge(bias_io.sem, 16 * 9)
            for h in range(HEADS):
                if h >= 4:
                    pe.wait_ge(bias_done.sem, h - 3)
                pe.matmul(bank[3 + h % 4][:, :], flip[:, :], work[:, h, :], start=True, stop=True).then_inc(bias_mm.sem, 1)
            pe.wait_ge(bias_done.sem, HEADS)

            def channels(s, ks):
                for k in ks:
                    if k >= 4:
                        pe.wait_ge(s.hf_done.sem, k - 3)
                    for t in range(ST):
                        mm = pe.transpose(bank[3 + k % 4][:, P * t:P * (t + 1)], z[:, t, P * k:P * (k + 1)], ident[:, :])
                    mm.then_inc(s.h_bank.sem, 1)

            pe.wait_ge(x_io.sem, 16)
            for chunk in range(4):
                channels(layers[0], range(4 * chunk, 4 * chunk + 4))
                pe.wait_ge(pro_used.sem, KT * (chunk + 1))
                for j in range(8):
                    mm = pe.matmul(bank[7][:, j:j + 1], ada_acc[:, j // 4, P * (j % 4):P * (j % 4 + 1)],
                                   ones[:, 0:1], start=True, stop=True)
                mm.then_inc(pro_sum.sem, 1)

            for l, s in enumerate(layers):
                pe.sem_inc(s.mm_done.sem, NHL)
                if l:
                    pe.wait_ge(layers[l - 1].xn.sem, ST)
                    channels(s, range(KT))

                def product(out_, xs, ws, first, last):
                    (xh, xl), (wh, wl) = xs, ws
                    pe.matmul(out_, xh, wh, start=first, stop=False)
                    pe.matmul(out_, xh, wl, start=False, stop=False)
                    return pe.matmul(out_, xl, wh, start=False, stop=last)

                with pe.Fori(0, CT) as ct:
                    def is_free(b, use):
                        pe.wait_ge(s.free[b].sem, s.free[b].at(use, ct))

                    def fill(b, mm):
                        mm.then_inc(s.full[b].sem, 1)

                    def s5_turn():
                        pe.wait_ge(s.bb_done.sem, s.bb_done.at(1, ct))
                        is_free(4, 0)
                        for i in range(2):
                            pe.transpose(bank[4][:, P * i:P * (i + 1)],
                                         s5_bb[:, i, :, :, :].rearrange("p a b c -> p (a b c)"), ident[:, :])
                        for i in range(2):
                            mm = pe.transpose(bank[4][:, P * (2 + i):P * (3 + i)],
                                              s5_cc[:, i, :, :].rearrange("p a b -> p (a b)"), ident[:, :])
                        fill(4, mm)

                    def s5_drive(q):
                        if q == 0:
                            unit_copied(pe, s, "d_u", ct)
                            is_free(4, 1)
                        for i in range(2):
                            is_free(2 + i, q)
                            fill(2 + i, pe.matmul(bank[2 + i][:, :], s5_w[32 * q:32 * q + 32, i, :],
                                                  u_d[32 * q:32 * q + 32, :], start=True, stop=True))

                    def s5_output(q):
                        pe.wait_ge(s.x_rot.sem, s.x_rot.at(q + 1, ct))
                        o = bank[4][32 * q:32 * q + 32, :]
                        pe.matmul(o, s5_w[:, 2, 32 * q:32 * q + 32], s5_s[3], start=True, stop=False)
                        mm = pe.matmul(o, s5_w[:, 3, 32 * q:32 * q + 32], s5_s[4], start=False, stop=True)
                        mm.then_inc(s.c_done.sem, 1)

                    def lru_gates():
                        pe.wait_ge(s.xc_done.sem, s.xc_done.at(1, ct))
                        pe.wait_ge(s.step_in.sem, s.step_in.at(160, ct))
                        pe.wait_ge(s.p_copy.sem, s.p_copy.at(0, ct))
                        for i in range(2):
                            is_free(5 + i, 0)
                            fill(5 + i, pe.matmul(bank[5 + i][:, :], lru_w[:, i, :], xc, start=True, stop=True))

                    def scores(h, t):
                        b = 5 + t % 2
                        if h == 0 and t == 0:
                            unit_copied(pe, s, "q", ct)
                            unit_copied(pe, s, "k", ct)
                            pe.wait_ge(s.step_in.sem, s.step_in.at(160, ct))
                        if h == 1:
                            pe.wait_ge(s.p_copy.sem, s.p_copy.at(ST, ct))
                        is_free(b, 1 + 2 * h + t // 2)
                        fill(b, pe.matmul(bank[b][:, 0:P * (t + 1)], q_t[64 * h:64 * h + 64, P * t:P * (t + 1)],
                                          k_t[64 * h:64 * h + 64, 0:P * (t + 1)], start=True, stop=True))

                    def p_turn(h, kb):
                        b = 5 + kb % 2
                        pe.wait_ge(s.p_norm.sem, s.p_norm.at(h + 1, ct))
                        if kb >= 2:
                            pe.wait_ge(s.p_copy.sem, s.p_copy.at(ST * h + kb - 1, ct))
                        for t in range(kb, ST):
                            mm = pe.transpose(bank[b][:, P * (t - kb):P * (t - kb + 1)],
                                              prob[:, P_AT[t] + P * kb:P_AT[t] + P * (kb + 1)], ident[:, :])
                        fill(b, mm)

                    def weigh(h, kb):
                        pe.wait_ge(s.p_copy.sem, s.p_copy.at(4 * h + kb + 1, ct))
                        if h == 0 and kb == 0:
                            is_free(7, 1)
                        pe.matmul(bank[7][64 * h:64 * h + 64, P * kb:S], v_s[:, kb, 64 * h:64 * h + 64],
                                  p_t[:, kb % 2, 0:P * (ST - kb)], start=kb == 0, stop=kb == ST - 1)\
                            .then_inc(s.pv_done.sem, 1)

                    def v_turn():
                        unit_copied(pe, s, "v", ct)
                        is_free(7, 0)
                        for t in range(ST):
                            mm = pe.transpose(bank[7][:, P * t:P * (t + 1)], v_t[:, P * t:P * (t + 1)], ident[:, :])
                        fill(7, mm)

                    def ada_sum():
                        pe.wait_ge(s.ada_used.sem, s.ada_used.at(s.ada, ct))
                        pe.wait_ge(s.p_copy.sem, s.p_copy.at(2 * ST, ct))
                        is_free(5, 5)
                        for i in range(len(ADA_CHUNKS[l])):
                            for j in range(4):
                                mm = pe.matmul(bank[5][:, 4 * i + j:4 * i + j + 1], ada_acc[:, i, P * j:P * (j + 1)],
                                               ones[:, 0:1], start=True, stop=True)
                        fill(5, mm)

                    between = [[] for _ in range(HALF)]

                    def put(n, part, *args):
                        between[n].append(lambda: part(*args))

                    put(3, s5_turn)
                    put(6, lru_gates)
                    for q, (at_drive, at_output) in enumerate(((5, 9), (7, 12), (10, 16), (13, 19))):
                        put(at_drive, s5_drive, q)
                        put(at_output, s5_output, q)
                    for h, at in ((0, 10), (1, 17)):
                        for t in range(ST):
                            put(at + t // 2, scores, h, t)
                    put(11, v_turn)
                    for h, at in ((0, 14), (1, 21)):
                        put(at, p_turn, h, 0)
                        put(at, p_turn, h, 1)
                        put(at + 1, weigh, h, 0)
                        put(at + 1, weigh, h, 1)
                        put(at + 1, p_turn, h, 2)
                        put(at + 1, p_turn, h, 3)
                        put(at + 2, weigh, h, 2)
                        put(at + 2, weigh, h, 3)
                    put(HALF - 1, ada_sum)

                    for n in range(HALF):
                        u, half = n // 2, n % 2
                        if half == 0:
                            is_free(u % 2, u // 2)
                        pe.wait_ge(s.lo_done.sem, s.lo_done.at(n + 1, ct))
                        for j in range(KH):
                            k = half * KH + j
                            if u == 0:
                                pe.wait_ge(s.op_lo.sem, k + 1)
                            w = slice(P * j, P * (j + 1))
                            mm = product(bank[u % 2][:, :], (w_hi[:, n % NHL, w], w_lo[:, n % NHL, w]),
                                         (op_hi[:, k, :], op_lo[:, k, :]), k == 0, k == KT - 1)
                        mm.then_inc(s.mm_done.sem, 1)
                        for part in between[n]:
                            part()

                pe.wait_ge(s.glu_in.sem, 16)
                pe.wait_ge(s.step_end.sem, s.step_end.at(0, CT))
                for m in range(4):
                    for k in range(4):
                        mm = pe.matmul(bank[4 + m][:, :], w_glu[:, k, P * m:P * (m + 1)], y_t[:, 12 + k, :],
                                       start=k == 0, stop=k == 3)
                    mm.then_inc(s.glu_mm.sem, 1)
                for c in range(4):
                    pe.wait_ge(s.diag.sem, c + 1)
                    pe.wait_ge(s.glu_t.sem, c + 1)
                    pe.matmul(bank[4 + c][:, :], ones[:, :], diag[:, c % 2, :], start=True, stop=True)\
                        .then_inc(s.gb_mm.sem, 1)
                for b in range(4):
                    pe.wait_ge(s.free[b].sem, s.free[b].at(0, CT))
                for n in range(W_OUT):
                    c, kk = n // 8, n % 8
                    if n == 8:
                        pe.wait_ge(s.gb.sem, 4)
                    pe.wait_ge(s.lo_done.sem, s.lo_done.at(n + 1, CT))
                    for t in range(ST):
                        if c >= 2 and kk == 0:
                            pe.wait_ge(s.y_used.sem, 4 * (c - 2) + t + 1)
                        for j in range(2):
                            k = 2 * kk + j
                            if c == 0 and t == 0:
                                pe.wait_ge(s.op_lo.sem, KT + k + 1)
                            x_, w_ = slice(P * t, P * (t + 1)), slice(S * j, S * (j + 1))
                            mm = product(bank[4 * (c % 2) + t][:, :], (op_hi[:, k, x_], op_lo[:, k, x_]),
                                         (w_hi[:, n % NHL, w_], w_lo[:, n % NHL, w_]), k == 0, k == KT - 1)
                        if kk == 7 and t < ST - 1:
                            mm.then_inc(s.y_mm.sem, 1)
                    mm.then_inc(s.mm_done.sem, 1)

        def branch_loop(dve, l, s, line, own, tt, ts, stt, repeat):
            ADD, SUB, MUL = ALU.add, ALU.subtract, ALU.mult
            pr = {name: at for name, (at, _) in ROWS.items()}
            with dve.Fori(0, CT) as ct:
                counted = [s.own, s.to_act, s.p_norm, s.x_rot, s.xc_done, s.bb_done, s.step_end,
                           *s.gate_used, *s.free, s.ada_used]
                line.enter(ct, *counted)
                for b, before in ((1, 5), (4, 1), (5, 1), (6, 1), (7, 1)):
                    s.free[b].local = before
                pieces = [0]

                def ada(*counts):
                    for _ in range(counts[l]):
                        a = pieces[0]
                        pieces[0] += 1
                        chunk, k = a // KT, a % KT
                        acc, src = ada_acc[:, chunk, :], ada_in[:, a % ADA_RING, :]
                        dve.wait_ge(s.ada_in[a % ADA_RING].sem, s.ada_in[a % ADA_RING].at(16 * (a // ADA_RING + 1), ct))
                        if k:
                            dve.wait_ge(s.ada_used.sem, s.ada_used.at(a, ct))
                            stt(acc, src, cond[:, k:k + 1], acc, MUL, ADD).then_inc(s.ada_used.sem, 1)
                        else:
                            ts(acc, src, cond[:, 0:1], MUL).then_inc(s.ada_used.sem, 1)

                def ada_read():
                    dve.wait_ge(s.full[5].sem, s.full[5].at(10, ct))
                    for i, (of, part) in enumerate(ADA_CHUNKS[l]):
                        to = bass.ds(ct * 4 + part, 4)
                        read = tt(ada_t[:, of, to], bank[5][:, 4 * i:4 * i + 4], ada_b[:, of, to], ADD)
                        if i == len(ADA_CHUNKS[l]) - 1:
                            read.then_inc(s.free[5].sem, 1)
                        else:
                            own(read, s.own)

                def col(name, k=0):
                    return par[:, l, bass.ds(ct + (pr[name] + k), 1)]

                def y_out(branch):
                    return y_t[:, bass.ds(ct + 4 * branch, 1), :].rearrange("p o t -> p (o t)")

                dve.wait_ge(s.step_in.sem, s.step_in.at(160, ct))
                own(dve.tensor_copy(s5_k[:, :, :], s5c[:, l, :, bass.ds(ct * SQ, SQ)]), s.own)
                turns = rot[:, 0, :, :]
                j_all = j_row[:, :].unsqueeze(1).to_broadcast([P, SQ, TC])
                own(tt(turns, repeat(s5_k[:, 1, :], TC), j_all, MUL), s.own)
                own(ts(rot[:, 1, :, :], turns, ROUND, ADD, ROUND, SUB), s.own)
                own(tt(turns, turns, rot[:, 1, :, :], SUB), s.own)
                own(stt(rot[:, 1, :, :], turns, -1.0, turns, MUL, ALU.max), s.to_act)
                ada(4, 1)
                for i in range(2):
                    for g in range(2):
                        c_in = s5_raw[:, 2 + i, :]
                        own(ts(s5_cc[:, i, g, :], c_in, mask[:, 2 * i + g:2 * i + g + 1], MUL), s.own)
                t1 = s5_s[2][:, 0:64].rearrange("p (s c) -> p s c", s=SQ)
                t2 = s5_s[2][:, 64:128].rearrange("p (s c) -> p s c", s=SQ)
                b_re, b_im = (s5_raw[:, i, :].rearrange("p (s c) -> p s c", s=SQ) for i in range(2))
                f_re, f_im = repeat(s5_k[:, 2, :], CH), repeat(s5_k[:, 3, :], CH)
                for i, (u_, v_, op) in enumerate(((b_re, b_im, SUB), (b_im, b_re, ADD))):
                    own(tt(t1, u_, f_re, MUL), s.own)
                    own(tt(t2, v_, f_im, MUL), s.own)
                    for g in range(2):
                        h = slice(64 * g, 64 * g + 64)
                        o = s5_bb[h, i, :, g, :]
                        op_ = tt(o, t1[h], t2[h], op)
                        if i == 1 and g == 1:
                            own(op_, s.bb_done)
                        else:
                            own(op_, s.own)
                ada(4, 1)

                unit_copied(dve, s, "c_x", ct)
                own(ts(xc, xp[:, 3:3 + S], col("conv_c", 12), MUL, col("conv_c_b"), ADD), s.own)
                for k in (2, 1):
                    own(stt(xc, xp[:, k:k + S], col("conv_c", 4 * k), xc, MUL, ADD), s.own)
                own(stt(xc, xp[:, 0:S], col("conv_c"), xc, MUL, ADD), s.xc_done)
                ada(4, 2)

                def s5_tile(q):
                    cos = rot[:, 1, q, :].unsqueeze(1).to_broadcast([P, 4, TC])
                    sin = rot[:, 0, q, :].unsqueeze(1).to_broadcast([P, 4, TC])
                    w_re, w_im, t_, x_re, x_im = (v.rearrange("p (a b) -> p a b", a=4) for v in s5_s)
                    if q == 0:
                        dve.wait_ge(s.from_act.sem, s.from_act.at(1, ct))
                    dve.wait_ge(s.full[2].sem, s.full[2].at(q + 1, ct))
                    dve.wait_ge(s.full[3].sem, s.full[3].at(q + 1, ct))
                    bu_re, bu_im = (bank[2 + i][:, :].rearrange("p (a b) -> p a b", a=4) for i in range(2))
                    own(tt(w_re, bu_re, cos, MUL), s.own)
                    own(tt(t_, bu_im, sin, MUL), s.own)
                    own(tt(w_re, w_re, t_, ADD), s.own)
                    own(tt(w_im, bu_im, cos, MUL), s.free[3])
                    own(tt(t_, bu_re, sin, MUL), s.free[2])
                    own(tt(w_im, w_im, t_, SUB), s.own)
                    mag = s5_k[:, 0, q:q + 1].to_broadcast([P, TC])
                    cl, sl = rot[:, 1, q, TC - 1:TC], rot[:, 0, q, TC - 1:TC]
                    for c in range(S // TC):
                        i_re, i_im = (0.0, 0.0) if c == 0 else (carry[:, 1:2], carry[:, 3:4])
                        a, b = (v[:, c * TC:(c + 1) * TC] for v in s5_s[0:2])
                        own(dve.tensor_tensor_scan(a, mag, a, i_re, MUL, ADD), s.own)
                        own(dve.tensor_tensor_scan(b, mag, b, i_im, MUL, ADD), s.own)
                        if c < S // TC - 1:
                            e_re, e_im = a[:, TC - 1:TC], b[:, TC - 1:TC]
                            own(tt(carry[:, 0:1], e_im, sl, MUL), s.own)
                            own(tt(carry[:, 2:3], e_im, cl, MUL), s.own)
                            own(stt(carry[:, 1:2], e_re, cl, carry[:, 0:1], MUL, SUB), s.own)
                            own(stt(carry[:, 3:4], e_re, sl, carry[:, 2:3], MUL, ADD), s.own)
                    dve.wait_ge(s.c_done.sem, s.c_done.at(q, ct))
                    own(tt(x_re, w_re, cos, MUL), s.own)
                    own(tt(t_, w_im, sin, MUL), s.own)
                    own(tt(x_re, x_re, t_, SUB), s.own)
                    own(tt(x_im, w_im, cos, MUL), s.own)
                    own(tt(t_, w_re, sin, MUL), s.own)
                    own(tt(x_im, x_im, t_, ADD), s.x_rot)

                def score_max(h, ts_):
                    for t in ts_:
                        b, use = 5 + t % 2, 1 + 4 * h + t // 2
                        w = P * (t + 1)
                        dve.wait_ge(s.full[b].sem, s.full[b].at(use + 1, ct))
                        line(dve.memset(spare[:, :], 0.0), s.own)
                        own(dve.tensor_tensor_reduce(prob[:, P_AT[t]:P_AT[t] + w], bank[b][:, 0:w],
                                                      bias_t[:, h, S - w:S], 1.0, -3e38, ADD, ALU.max,
                                                      soft[:, 0, t:t + 1]), s.free[b])
                    if ts_[-1] == 3:
                        own(ts(soft[:, 1, :], soft[:, 0, :], -1.0, MUL), s.to_act)

                def normalise(h):
                    dve.wait_ge(s.from_act.sem, s.from_act.at(3 + h, ct))
                    own(dve.reciprocal(soft[:, 3, :], soft[:, 2, :]), s.own)
                    for t in range(ST):
                        pt = prob[:, P_AT[t]:P_AT[t] + P * (t + 1)]
                        own(ts(pt, pt, soft[:, 3, t:t + 1], MUL), s.own if t < 3 else s.p_norm)

                def silu2(i, use_name, dst):
                    unit_copied(dve, s, use_name, ct)
                    return stt(dst, gt[:, i, :], 1.0, gx[:, i, :], ADD, MUL)

                s5_tile(0)
                dve.wait_ge(s.from_act.sem, s.from_act.at(2, ct))
                own(ts(lru_s[0], lru_s[0], 1.0, ADD), s.own)
                own(dve.reciprocal(lru_s[0], lru_s[0]), s.own)
                own(tt(lru_s[2], lru_s[2], lru_s[0], MUL), s.own)
                own(ts(lru_s[0], lru_s[0], 2.0, MUL, -1.0, ADD), s.own)
                own(stt(lru_s[1], lru_s[1], 1.0, xc, ADD, MUL), s.own)
                own(tt(lru_s[1], lru_s[1], lru_s[2], MUL), s.own)
                own(dve.tensor_tensor_scan(xc, lru_s[0], lru_s[1], 0.0, MUL, ADD), s.own)
                ada(3, 1)
                s5_tile(1)
                score_max(0, (0, 1))
                ada(1, 1)
                score_max(0, (2, 3))
                ada(4, 1)
                normalise(0)
                s5_tile(2)
                own(silu2(0, "c_g", gx[:, 0, :]), s.own)
                dve.wait_ge(x_io.sem, 16 * (1 + (ST if l else 0)))
                own(stt(y_out(2), xc, 0.5, gx[:, 0, :], MUL, MUL), s.gate_used[0])
                s5_tile(3)
                ada(2, 1)
                score_max(1, (0, 1))
                ada(5, 2)
                score_max(1, (2, 3))
                own(silu2(1, "d_g", silu_d[:, bass.ds(ct, 1), :].rearrange("p o t -> p (o t)")), s.gate_used[1])
                ada(6, 2)
                normalise(1)
                y = s5_s[0]
                dve.wait_ge(s.c_done.sem, s.c_done.at(SQ, ct))
                own(stt(y, u_d, col("s5_d"), bank[4][:, :], MUL, ADD), s.free[4])
                own(tt(s5_s[2], y, y, MUL), s.own)
                own(ts(s5_s[2], s5_s[2], 0.044715, MUL, 1.0, ADD), s.own)
                own(tt(gel, s5_s[2], y, MUL), s.to_act)
                ada(15, 4)
                unit_copied(dve, s, "a_x", ct)
                v = va[:, 2:2 + S]
                own(tt(v, v, ax, MUL), s.own)
                cv = s5_s[1]
                own(ts(cv, v, col("conv_a", 8), MUL), s.own)
                own(stt(cv, va[:, 1:1 + S], col("conv_a", 4), cv, MUL, ADD), s.own)
                own(stt(cv, va[:, 0:S], col("conv_a"), cv, MUL, ADD), s.own)
                own(silu2(0, "b_g", gx[:, 0, :]), s.own)
                dve.wait_ge(s.pv_done.sem, s.pv_done.at(2 * ST, ct))
                own(stt(s5_s[2], bank[7][:, :], 0.5, gx[:, 0, :], MUL, MUL), s.free[7])
                own(dve.tensor_copy(y_out(1), s5_s[2]), s.gate_used[0])
                own(silu2(1, "a_g", gx[:, 1, :]), s.own)
                dve.wait_ge(s.mm_done.sem, s.mm_done.at(HALF, ct))
                own(tt(cv, cv, bank[1][:, :], MUL), s.free[1])
                own(stt(y_out(0), cv, 0.5, gx[:, 1, :], MUL, MUL), s.gate_used[1])
                ada_read()
                dve.wait_ge(s.from_act.sem, s.from_act.at(5, ct))
                own(stt(y, gel, 1.0, y, ADD, MUL), s.own)
                own(ts(y_out(3), y, 0.5, MUL), s.step_end)
                assert s.own.local == s.own.per, s.own.local
                assert pieces[0] == s.ada, pieces[0]
                for sig in counted:
                    sig.local = 0
                line.step = CT
            line.last = None

        @block.vector
        def _(dve):
            line = Line(dve)

            def own(ins, sig):
                line(ins, sig)
                line.settle()

            def tt(o, a, b, op):
                return dve.tensor_tensor(o, a, b, op)

            def ts(o, a, s1, op0, s2=None, op1=None):
                if op1 is None:
                    return dve.tensor_scalar(o, a, s1, None, op0)
                return dve.tensor_scalar(o, a, s1, s2, op0, op1)

            def stt(o, a, sc, b, op0, op1):
                return dve.scalar_tensor_tensor(o, a, sc, b, op0, op1)

            def repeat(col, n):
                return col.unsqueeze(2).to_broadcast([col.shape[0], col.shape[1], n])

            ADD, SUB, MUL = ALU.add, ALU.subtract, ALU.mult
            dt_done = Signal(setup_own.sem, 0, 0)
            steps = Signal(setup_dve.sem, 0, 0)

            dve.wait_ge(const_done.sem, 14)
            for s in layers:
                dve.sem_inc(s.ada_used.sem, ADA_RING)
            sched = Signal(param_own.sem, 0, 0)
            own(dve.tensor_copy(j_row[:, :], j_int[:, :]), sched)
            def repeat_dt(l):
                dve.wait_ge(row_dma[l].sem, 16 * 15)
                line(dve.tensor_copy(dt_row[l][:, :].rearrange("s (g p) -> s g p", g=2), repeat(dt_in[:, l, :], NS)),
                     dt_done)

            def parameters(l):
                dve.wait_ge(turned.sem, 3 + 4 * l if l else 4)
                own(dve.tensor_copy(par[:, l, :], bank[0][:, 0:N_ROWS]), sched)
                own(dve.tensor_copy(ada_b[:, l, :], bank[1][:, 0:64]), sched)
                if l == 0:
                    own(dve.tensor_copy(mask[:, 0:1], bank[3][:, 0:1]), sched)
                    own(ts(mask[:, 1:2], mask[:, 0:1], -1.0, MUL, 1.0, ADD), sched)
                    own(ts(mask[:, 2:4], mask[:, 0:2], -1.0, MUL), sched)
                    line(dve.tensor_copy(gate1[:, :], ada_b[:, 0, 48:64]), steps)
                    dve.wait_ge(setup_act.sem, 1)
                    line.settle()
                    own(stt(cond[:, :], cond[:, :], 1.0, gate1[:, :], ADD, MUL), sched)
                    own(ts(cond[:, :], cond[:, :], 0.5, MUL), sched)
                line(dve.tensor_copy(dt_t[:, l, :], bank[2][:, 0:16]), steps)
                dve.wait_ge(setup_act.sem, 7 * l + 2)
                lam = ROWS["s5_lam_re"][0]
                re, im, dt = par[:, l, lam:lam + 16], par[:, l, lam + 16:lam + 32], dt_t[:, l, :]
                lru = ROWS["lru_lambda"][0]
                lrl = par[:, l, lru:lru + 4]
                own(tt(tmp[:, 0, :], re, dt, MUL), sched)
                own(tt(tmp[:, 1, :], im, dt, MUL), sched)
                own(ts(tmp[:, 1, :], tmp[:, 1, :], 1 / (2 * math.pi), MUL), sched)
                own(ts(tmp[:, 7, :], tmp[:, 1, :], ROUND, ADD, ROUND, SUB), sched)
                own(tt(tmp[:, 1, :], tmp[:, 1, :], tmp[:, 7, :], SUB), sched)
                own(dve.tensor_copy(s5c[:, l, 1, :], tmp[:, 1, :]), sched)
                own(ts(tmp[:, 2, 0:4], lrl, -1.0, MUL), sched)
                own(ts(tmp[:, 2, 4:8], tmp[:, 2, 0:4], 0.0, ALU.max), sched)
                own(tt(tmp[:, 2, 8:12], tmp[:, 2, 0:4], lrl, ALU.min), sched)
                line(dve.tensor_copy(tmp[:, 2, 0:4], tmp[:, 2, 8:12]), steps)
                dve.wait_ge(setup_act.sem, 7 * l + 6)
                line(ts(tmp[:, 3, 0:4], tmp[:, 2, 0:4], 1.0, ADD), steps)
                own(ts(tmp[:, 7, :], tmp[:, 0, :], -1.0, MUL, 1.0, ADD), sched)
                own(dve.reciprocal(tmp[:, 7, :], tmp[:, 7, :]), sched)
                own(stt(tmp[:, 0, :], tmp[:, 0, :], 2.0, tmp[:, 7, :], MUL, MUL), sched)
                own(ts(s5c[:, l, 0, :], tmp[:, 0, :], 1.0, ADD), sched)
                own(tt(tmp[:, 6, :], tmp[:, 6, :], tmp[:, 6, :], MUL), sched)
                own(stt(tmp[:, 6, :], tmp[:, 6, :], -2.0, s5c[:, l, 0, :], MUL, MUL), sched)
                own(tt(tmp[:, 0, :], tmp[:, 0, :], tmp[:, 6, :], ADD), sched)
                own(tt(tmp[:, 5, :], tmp[:, 5, :], s5c[:, l, 0, :], MUL), sched)
                own(tt(tmp[:, 6, :], re, re, MUL), sched)
                own(tt(tmp[:, 7, :], im, im, MUL), sched)
                own(tt(tmp[:, 7, :], tmp[:, 7, :], tmp[:, 6, :], ADD), sched)
                own(dve.reciprocal(tmp[:, 7, :], tmp[:, 7, :]), sched)
                own(tt(tmp[:, 6, :], tmp[:, 0, :], re, MUL), sched)
                own(tt(tmp[:, 1, :], tmp[:, 5, :], im, MUL), sched)
                own(tt(tmp[:, 6, :], tmp[:, 6, :], tmp[:, 1, :], ADD), sched)
                own(tt(s5c[:, l, 2, :], tmp[:, 6, :], tmp[:, 7, :], MUL), sched)
                own(tt(tmp[:, 6, :], tmp[:, 5, :], re, MUL), sched)
                own(tt(tmp[:, 1, :], tmp[:, 0, :], im, MUL), sched)
                own(tt(tmp[:, 6, :], tmp[:, 6, :], tmp[:, 1, :], SUB), sched)
                own(tt(s5c[:, l, 3, :], tmp[:, 6, :], tmp[:, 7, :], MUL), sched)
                dve.wait_ge(setup_act.sem, 7 * l + 8)
                own(ts(tmp[:, 4, 4:8], tmp[:, 4, 0:4], -1.0, MUL, 1.0, ADD), sched)
                own(dve.reciprocal(tmp[:, 4, 4:8], tmp[:, 4, 4:8]), sched)
                own(stt(tmp[:, 4, 0:4], tmp[:, 4, 0:4], 2.0, tmp[:, 4, 4:8], MUL, MUL), sched)
                own(tt(tmp[:, 4, 4:8], tmp[:, 2, 0:4], tmp[:, 4, 0:4], SUB), sched)
                own(ts(tmp[:, 4, 0:4], tmp[:, 4, 0:4], 1.0, ADD), sched)
                own(dve.reciprocal(tmp[:, 4, 0:4], tmp[:, 4, 0:4]), sched)
                own(tt(tmp[:, 4, 4:8], tmp[:, 4, 4:8], tmp[:, 4, 0:4], MUL), sched)
                own(tt(tmp[:, 3, 0:4], tmp[:, 3, 0:4], tmp[:, 4, 4:8], ADD), sched)
                own(tt(tmp[:, 3, 0:4], tmp[:, 3, 0:4], tmp[:, 2, 4:8], ADD), sched)
                own(ts(lru_c[:, l, 0:4], tmp[:, 3, 0:4], LRU_C / 4, MUL), sched)
                r = ROWS["lru_ba"][0]
                own(ts(lru_c[:, l, 4:12], par[:, l, r:r + 8], 0.5, MUL), sched)
                r = ROWS["s5_b_glu"][0]
                own(ts(glu_hb[:, l, :], par[:, l, r:r + 4], 0.5, MUL), sched)

            repeat_dt(0)
            parameters(0)
            repeat_dt(1)

            def modulated(s, ks):
                for k in ks:
                    dve.wait_ge(s.h_bank.sem, k + 1)
                    if k >= 2:
                        dve.wait_ge(s.op_hi.sem, k - 1)
                        dve.wait_ge(s.op_lo.sem, k - 1)
                    dve.tensor_scalar(hf[:, k % 2, :], bank[3 + k % 4][:, :], hs[:, 0, k:k + 1], hs[:, 1, k:k + 1],
                                      MUL, ADD).then_inc(s.hf_done.sem, 1)

            acc = ada_acc[:, 0:2, :]
            for chunk in range(4):
                for k in range(KT):
                    a = KT * chunk + k
                    dve.wait_ge(pro_in[a % PRO_RING].sem, 16 * (a // PRO_RING + 1))
                    if k:
                        dve.wait_ge(pro_used.sem, a)
                        op = stt(acc, pro_ring[a % PRO_RING], cond[:, k:k + 1], acc, MUL, ADD)
                    else:
                        op = ts(acc, pro_ring[a % PRO_RING], cond[:, 0:1], MUL)
                    op.then_inc(pro_used.sem, 1)
                    if chunk and k % 4 == 3:
                        modulated(layers[0], [4 * (chunk - 1) + k // 4])
                dve.wait_ge(pro_sum.sem, chunk + 1)
                w, sums = slice(4 * chunk, 4 * chunk + 4), bank[7]
                own(tt(hs[:, 1, w], sums[:, 0:4], ada_b[:, 0, w], ADD), sched)
                own(stt(hs[:, 0, w], sums[:, 4:8], 1.0, ada_b[:, 0, 16 + 4 * chunk:20 + 4 * chunk], ADD, ADD), sched)
                if chunk == 0:
                    parameters(1)
            modulated(layers[0], range(KT - 4, KT))

            for l, s in enumerate(layers):
                pre = Signal(s.pre.sem, 0, 0)
                if l:
                    g, b = ROWS["ln_g"][0], ROWS["ln_b"][0]
                    own(ts(hs[:, 0, :], ada_t[:, l, 16:32], 1.0, ADD), pre)
                    own(tt(hs[:, 1, :], par[:, l - 1, b:b + 16], hs[:, 0, :], MUL), pre)
                    own(tt(hs[:, 1, :], hs[:, 1, :], ada_t[:, l, 0:16], ADD), pre)
                    own(tt(hs[:, 0, :], par[:, l - 1, g:g + 16], hs[:, 0, :], MUL), pre)
                    modulated(s, range(KT))
                dve.wait_ge(s.op_lo.sem, KT)
                dve.wait_ge(s.op_hi.sem, KT)

                branch_loop(dve, l, s, line, own, tt, ts, stt, repeat)

                post = Signal(s.post.sem, 0, 0)
                own(ts(gate1[:, :], ada_t[:, l, 32:48], 1.0, ADD), post)
                for c in range(4):
                    if c >= 2:
                        dve.wait_ge(s.gb_mm.sem, c - 1)
                    tt(diag[:, c % 2, :].rearrange("p (a b) -> p a b", a=4),
                       ident[:, :].unsqueeze(1).to_broadcast([P, 4, P]),
                       repeat(gate1[:, 4 * c:4 * c + 4], P), MUL).then_inc(s.diag.sem, 1)
                    for k in range(3 * c, 3 * c + 3):
                        dve.wait_ge(s.op_hi.sem, KT + k + 1)
                        tt(op_lo[:, k, :], y_t[:, k, :], op_hi[:, k, :].bitcast(F32), SUB).then_inc(s.op_lo.sem, 1)
                dve.wait_ge(s.glu_mm.sem, 4)
                for m in range(4):
                    dve.wait_ge(s.glu_t.sem, m + 1)
                    own(stt(glu_t[:, m, :], glu_t[:, m, :], 1.0, y_t[:, 12 + m, :], ADD, MUL), post)
                    stt(y_t[:, 12 + m, :], glu_t[:, m, :], 0.25, silu_d[:, m, :], MUL, MUL).then_inc(s.d_done.sem, 1)
                for k in range(12, 16):
                    dve.wait_ge(s.op_hi.sem, KT + k + 1)
                    tt(op_lo[:, k, :], y_t[:, k, :], op_hi[:, k, :].bitcast(F32), SUB).then_inc(s.op_lo.sem, 1)

                dve.wait_ge(s.gb.sem, 4)
                dve.wait_ge(s.z_in.sem, 16 * (ST + (2 if l else 0)))
                for c in range(4):
                    w = slice(S * c, S * (c + 1))
                    if l:
                        for t in range(ST):
                            own(tt(z[:, t, w], z[:, t, w], ln_prev[:, 0, w], MUL), post)
                            own(tt(z[:, t, w], z[:, t, w], ln_prev[:, 1, w], ADD), post)
                    for t in range(ST):
                        if t < ST - 1:
                            dve.wait_ge(s.y_mm.sem, 3 * c + t + 1)
                        else:
                            dve.wait_ge(s.mm_done.sem, s.mm_done.at(8 * (c + 1), CT))
                        tt(mix, bank[4 * (c % 2) + t][:, :], gate_b[:, c, :], MUL).then_inc(s.y_used.sem, 1)
                        dve.wait_ge(s.y_used.sem, 4 * c + t + 1)
                        own(stt(z[:, t, w], z[:, t, w], ALPHA, mix, MUL, ADD), post)
                        own(dve.bn_stats(stats[:, t, c, :], z[:, t, w]), post)
                        if c == 3:
                            line(dve.bn_aggr(mv[:, t, 0:2], stats[:, t, :, :]), s.var)
                if l == DEPTH - 1:
                    dve.wait_ge(s.ln_in.sem, 16 * 2)
                for t in range(ST):
                    dve.wait_ge(s.std.sem, t + 1)
                    own(dve.reciprocal(mv[:, t, 3:4], mv[:, t, 2:3]), post)
                    if l < DEPTH - 1:
                        norm = ts(z[:, t, :], z[:, t, :], mv[:, t, 0:1], SUB, mv[:, t, 3:4], MUL)
                    else:
                        own(stt(z[:, t, :], z[:, t, :], mv[:, t, 0:1], ln_last[:, 0, :], SUB, MUL), post)
                        norm = stt(z[:, t, :], z[:, t, :], mv[:, t, 3:4], ln_last[:, 1, :], MUL, ADD)
                    norm.then_inc(s.xn.sem, 1)
                dve.wait_ge(s.xn.sem, ST)


_INS = ("x", "c", "rel_bias", "w_ada", "b_ada", "w_in", "conv_a", "conv_c", "conv_c_b", "lru_wa", "lru_ba",
        "lru_wx", "lru_bx", "lru_lambda", "s5_lam_re", "s5_lam_im", "s5_log_dt", "s5_b_re", "s5_b_im",
        "s5_c_re", "s5_c_im", "s5_d", "s5_w_glu", "s5_b_glu", "w_out", "ln_g", "ln_b")


def kernel(**inputs):
    import concourse.bacc as bacc
    from concourse.bass_utils import run_bass_kernel_spmd

    nc = bacc.Bacc("TRN2", target_bir_lowering=False, num_devices=1)
    arrays, drams = {}, {}
    for name in _INS:
        a = np.ascontiguousarray(inputs[name])
        arrays["in_" + name] = a
        drams[name] = nc.dram_tensor("in_" + name, a.shape, mybir.dt.from_np(a.dtype), kind="ExternalInput").ap()
    out = nc.dram_tensor("out", (1, S, D), F32, kind="ExternalOutput").ap()
    trunk(nc, drams, out)
    return run_bass_kernel_spmd(nc, [arrays], core_ids=[0]).results[0]["out"]
```
